# Optimizing a Trainium2 kernel written in Bass

```python
import math
import jax, jax.numpy as jnp
from jax import lax
import numpy as np

D_MODEL = 1024
BATCH = 1
SEQ = 256
DEPTH = 2

GRID_W = 64
N_MIXERS = 3
N_A = len(range(0, DEPTH, N_MIXERS))
N_B = len(range(1, DEPTH, N_MIXERS))
N_C = len(range(2, DEPTH, N_MIXERS))

NA_HEADS = 16
NA_HEAD_DIM = D_MODEL // NA_HEADS
NA_KH = 8
NA_KW = 16

MLA_HEADS = 16
MLA_NOPE = 64
MLA_ROPE = 32
MLA_V = D_MODEL // MLA_HEADS
MLA_Q_RANK = 256
MLA_KV_RANK = 256
ROPE_THETA = 10000.0
Q_BLOCK = 128

HG_EXPAND = 128
HG_HEADS = D_MODEL // HG_EXPAND
HG_F = HG_EXPAND
HG_V = D_MODEL // HG_HEADS
HG_CHUNK = 64

PEER_HEADS = 8
PEER_NKEYS = 128
PEER_EXPERTS = PEER_NKEYS * PEER_NKEYS
PEER_DK = 256
PEER_TOPK = 16
PEER_TOK_BLOCK = 128

NORM_EPS = 1e-5
DN_ALPHA = (2.0 * DEPTH) ** 0.25
DN_BETA = (8.0 * DEPTH) ** -0.25

kernel_name = 'hybrid_natten_mla_hgrn2_peer_encoder'

F32 = jnp.float32

def layer_norm(x, g, b):
    xf = x.astype(F32)
    mu = jnp.mean(xf, axis=-1, keepdims=True)
    var = jnp.mean(jnp.square(xf - mu), axis=-1, keepdims=True)
    return ((xf - mu) * lax.rsqrt(var + NORM_EPS) * g.astype(F32) + b.astype(F32)).astype(x.dtype)

def rms_norm(x, g):
    xf = x.astype(F32)
    y = xf * lax.rsqrt(jnp.mean(jnp.square(xf), axis=-1, keepdims=True) + NORM_EPS)
    return (y * g.astype(F32)).astype(x.dtype)

def neighborhood_attention(x, w_in, rel_bias, w_out):
    B, S, D = x.shape
    rows = S // GRID_W
    kh = min(NA_KH, rows)
    qkv = (x @ w_in).reshape(B, rows, GRID_W, 3, NA_HEADS, NA_HEAD_DIM)
    q = qkv[:, :, :, 0] * (NA_HEAD_DIM ** -0.5)
    k = qkv[:, :, :, 1]
    v = qkv[:, :, :, 2]
    cols = np.arange(GRID_W)
    c0 = np.clip(cols - NA_KW // 2, 0, GRID_W - NA_KW)
    col_idx = c0[:, None] + np.arange(NA_KW)[None, :]
    dc = col_idx - cols[:, None] + (NA_KW - 1)
    bias_c = rel_bias[:, :, dc]

    def row_step(r):
        r0 = jnp.clip(r - kh // 2, 0, rows - kh)
        k_rows = lax.dynamic_slice_in_dim(k, r0, kh, axis=1)
        v_rows = lax.dynamic_slice_in_dim(v, r0, kh, axis=1)
        k_win = k_rows[:, :, col_idx]
        v_win = v_rows[:, :, col_idx]
        q_row = lax.dynamic_index_in_dim(q, r, axis=1, keepdims=False)
        dr = r0 + jnp.arange(kh) - r + (NA_KH - 1)
        bias = jnp.take(bias_c, dr, axis=1).transpose(0, 2, 1, 3)
        s = jnp.einsum('bqhd,bkqjhd->bhqkj', q_row, k_win).astype(F32) + bias[None].astype(F32)
        p = jax.nn.softmax(s.reshape(B, NA_HEADS, GRID_W, kh * NA_KW), axis=-1)
        p = p.reshape(s.shape).astype(v.dtype)
        return jnp.einsum('bhqkj,bkqjhd->bqhd', p, v_win)

    o = lax.map(row_step, jnp.arange(rows))
    o = o.transpose(1, 0, 2, 3, 4).reshape(B, S, D)
    return o @ w_out

def apply_rope(x, cos, sin):
    half = x.shape[-1] // 2
    c = cos[None, :, None, :]
    s = sin[None, :, None, :]
    x1, x2 = x[..., :half], x[..., half:]
    return jnp.concatenate([x1 * c - x2 * s, x1 * s + x2 * c], axis=-1)

def mla_attention(x, w_in, q_norm, kv_norm, w_q_up, w_kv_up, w_out):
    B, S, D = x.shape
    dq = MLA_NOPE + MLA_ROPE
    h = x @ w_in
    cq = h[..., :MLA_Q_RANK]
    ckv = h[..., MLA_Q_RANK:MLA_Q_RANK + MLA_KV_RANK]
    k_pe = h[..., MLA_Q_RANK + MLA_KV_RANK:][:, :, None, :]
    q = (rms_norm(cq, q_norm) @ w_q_up).reshape(B, S, MLA_HEADS, dq)
    kv = (rms_norm(ckv, kv_norm) @ w_kv_up).reshape(B, S, MLA_HEADS, MLA_NOPE + MLA_V)
    half = MLA_ROPE // 2
    inv_freq = ROPE_THETA ** (-jnp.arange(half, dtype=F32) * 2.0 / MLA_ROPE)
    ang = jnp.arange(S, dtype=F32)[:, None] * inv_freq[None, :]
    cos = jnp.cos(ang).astype(x.dtype)
    sin = jnp.sin(ang).astype(x.dtype)
    q_pe = apply_rope(q[..., MLA_NOPE:], cos, sin)
    k_pe = apply_rope(k_pe, cos, sin)
    q = jnp.concatenate([q[..., :MLA_NOPE], q_pe], axis=-1) * (dq ** -0.5)
    k = jnp.concatenate([kv[..., :MLA_NOPE], jnp.broadcast_to(k_pe, (B, S, MLA_HEADS, MLA_ROPE))], axis=-1)
    v = kv[..., MLA_NOPE:]
    nb = S // Q_BLOCK
    qb = q.reshape(B, nb, Q_BLOCK, MLA_HEADS, dq).transpose(1, 0, 2, 3, 4)

    def block(qi):
        s = jnp.einsum('bqhd,bkhd->bhqk', qi, k).astype(F32)
        p = jax.nn.softmax(s, axis=-1).astype(v.dtype)
        return jnp.einsum('bhqk,bkhv->bqhv', p, v)

    o = lax.map(block, qb)
    o = o.transpose(1, 0, 2, 3, 4).reshape(B, S, MLA_HEADS * MLA_V)
    return o @ w_out

def hgrn2_chunk_scan(q, k, v, log_f):
    B, S, H, F = q.shape
    V = v.shape[-1]
    n = S // HG_CHUNK

    def to_chunks(a):
        return a.reshape(B, n, HG_CHUNK, H, a.shape[-1]).transpose(1, 0, 3, 2, 4)

    lower = jnp.tril(jnp.ones((HG_CHUNK, HG_CHUNK), dtype=bool))[None, None, :, :, None]

    def step(state, inp):
        qc, kc, vc, lc = inp
        b = jnp.cumsum(lc, axis=2)
        diff = b[:, :, :, None, :] - b[:, :, None, :, :]
        decay = jnp.exp(jnp.where(lower, diff, -jnp.inf))
        attn = jnp.einsum('bhtf,bhsf,bhtsf->bhts', qc, kc, decay)
        o = jnp.einsum('bhts,bhsv->bhtv', attn, vc) + jnp.einsum('bhtf,bhfv->bhtv', qc * jnp.exp(b), state)
        b_last = b[:, :, -1:, :]
        state = jnp.exp(b_last[:, :, 0, :])[..., None] * state + jnp.einsum('bhsf,bhsv->bhfv', kc * jnp.exp(b_last - b), vc)
        return state, o

    init = jnp.zeros((B, H, F, V), q.dtype)
    _, o = lax.scan(step, init, (to_chunks(q), to_chunks(k), to_chunks(v), to_chunks(log_f)))
    return o.transpose(1, 0, 3, 2, 4).reshape(B, S, H, V)

def hgrn2_mixer(x, w_in, lower_bound, norm_g, w_out):
    B, S, D = x.shape
    zq, zf_fwd, zf_bwd, zi, zg = jnp.split(x @ w_in, 5, axis=-1)

    def heads(a, d):
        return a.reshape(B, S, HG_HEADS, d).astype(F32)

    q = jax.nn.silu(heads(zq, HG_F))
    i = heads(zi, HG_V)
    lb = lower_bound.astype(F32).reshape(2, HG_HEADS, HG_F)

    def gates(z, lb_d):
        zf = heads(z, HG_F)
        f = lb_d + (1.0 - lb_d) * jax.nn.sigmoid(zf)
        return (1.0 - lb_d) * jax.nn.sigmoid(-zf), jnp.log(f)

    k_f, lf_f = gates(zf_fwd, lb[0])
    k_b, lf_b = gates(zf_bwd, lb[1])
    o_fwd = hgrn2_chunk_scan(q, k_f, i, lf_f)
    rev = lambda a: jnp.flip(a, axis=1)
    o_bwd = rev(hgrn2_chunk_scan(rev(q), rev(k_b), rev(i), rev(lf_b)))
    o = o_fwd + o_bwd
    o = o * lax.rsqrt(jnp.mean(jnp.square(o), axis=-1, keepdims=True) + NORM_EPS)
    o = o * norm_g.astype(F32).reshape(HG_HEADS, HG_V) * jax.nn.silu(heads(zg, HG_V))
    return o.reshape(B, S, D).astype(x.dtype) @ w_out

def peer_ffn(x, w_q, sub_keys, u, v):
    B, S, D = x.shape
    q = (x @ w_q).reshape(B, S, PEER_HEADS, 2, PEER_DK // 2)
    s = jnp.einsum('bshcd,cnd->bshcn', q, sub_keys).astype(F32)
    sv, si = lax.top_k(s, PEER_TOPK)
    cand_s = (sv[..., 0, :, None] + sv[..., 1, None, :]).reshape(B, S, PEER_HEADS, PEER_TOPK * PEER_TOPK)
    cand_i = (si[..., 0, :, None] * PEER_NKEYS + si[..., 1, None, :]).reshape(B, S, PEER_HEADS, PEER_TOPK * PEER_TOPK)
    best_s, pos = lax.top_k(cand_s, PEER_TOPK)
    e_idx = jnp.take_along_axis(cand_i, pos, axis=-1)
    gate = jax.nn.softmax(best_s, axis=-1).astype(x.dtype)
    n_tok = B * S
    nb = n_tok // PEER_TOK_BLOCK
    e_per = PEER_HEADS * PEER_TOPK
    xb = x.reshape(nb, PEER_TOK_BLOCK, D)
    eb = e_idx.reshape(nb, PEER_TOK_BLOCK, e_per)
    gb = gate.reshape(nb, PEER_TOK_BLOCK, e_per)

    def block(args):
        xt, et, gt = args
        hid = jax.nn.gelu(jnp.einsum('td,ted->te', xt, u[et]), approximate=False)
        return jnp.einsum('te,ted->td', gt * hid, v[et])

    y = lax.map(block, (xb, eb, gb))
    return y.reshape(B, S, D)

def setup_inputs(seed: int = 0) -> dict:
    key = jax.random.key(seed)
    ks = jax.random.split(key, 24)
    nrm = lambda k, shape, scale: jax.random.normal(k, shape, F32) * scale
    D = D_MODEL
    return {
        'x': nrm(ks[0], (BATCH, SEQ, D), 1.0),
        'na_w_in': nrm(ks[1], (N_A, D, 3 * D), D ** -0.5),
        'na_rel_bias': nrm(ks[2], (N_A, NA_HEADS, 2 * NA_KH - 1, 2 * NA_KW - 1), 0.1),
        'na_w_out': nrm(ks[3], (N_A, D, D), DN_BETA * D ** -0.5),
        'mla_w_in': nrm(ks[4], (N_B, D, MLA_Q_RANK + MLA_KV_RANK + MLA_ROPE), D ** -0.5),
        'mla_q_norm': 1.0 + nrm(ks[5], (N_B, MLA_Q_RANK), 0.01),
        'mla_kv_norm': 1.0 + nrm(ks[6], (N_B, MLA_KV_RANK), 0.01),
        'mla_w_q_up': nrm(ks[7], (N_B, MLA_Q_RANK, MLA_HEADS * (MLA_NOPE + MLA_ROPE)), MLA_Q_RANK ** -0.5),
        'mla_w_kv_up': nrm(ks[8], (N_B, MLA_KV_RANK, MLA_HEADS * (MLA_NOPE + MLA_V)), MLA_KV_RANK ** -0.5),
        'mla_w_out': nrm(ks[9], (N_B, MLA_HEADS * MLA_V, D), DN_BETA * (MLA_HEADS * MLA_V) ** -0.5),
        'hg_w_in': nrm(ks[10], (N_C, D, 5 * D), D ** -0.5),
        'hg_lower_bound': nrm(ks[11], (DEPTH, 2, D), 0.1),
        'hg_norm': 1.0 + nrm(ks[12], (N_C, D), 0.01),
        'hg_w_out': nrm(ks[13], (N_C, D, D), DN_BETA * D ** -0.5),
        'peer_w_q': nrm(ks[14], (DEPTH, D, PEER_HEADS * PEER_DK), D ** -0.5),
        'peer_sub_keys': nrm(ks[15], (DEPTH, 2, PEER_NKEYS, PEER_DK // 2), (PEER_DK // 2) ** -0.5),
        'peer_u': nrm(ks[16], (DEPTH, PEER_EXPERTS, D), D ** -0.5),
        'peer_v': nrm(ks[17], (DEPTH, PEER_EXPERTS, D), DN_BETA * PEER_HEADS ** -0.5),
        'ln_mix_g': 1.0 + nrm(ks[18], (DEPTH, D), 0.01),
        'ln_mix_b': nrm(ks[19], (DEPTH, D), 0.01),
        'ln_ffn_g': 1.0 + nrm(ks[20], (DEPTH, D), 0.01),
        'ln_ffn_b': nrm(ks[21], (DEPTH, D), 0.01),
    }

def reference(x, na_w_in, na_rel_bias, na_w_out, mla_w_in, mla_q_norm, mla_kv_norm, mla_w_q_up, mla_w_kv_up, mla_w_out, hg_w_in, hg_lower_bound, hg_norm, hg_w_out, peer_w_q, peer_sub_keys, peer_u, peer_v, ln_mix_g, ln_mix_b, ln_ffn_g, ln_ffn_b):
    lb_w = jax.nn.softmax(hg_lower_bound.astype(F32), axis=0)
    lb_all = jnp.cumsum(lb_w, axis=0) - lb_w[0:1]
    h = x
    for layer in range(DEPTH):
        kind = layer % N_MIXERS
        j = layer // N_MIXERS
        if kind == 0:
            mix = neighborhood_attention(h, na_w_in[j], na_rel_bias[j], na_w_out[j])
        elif kind == 1:
            mix = mla_attention(h, mla_w_in[j], mla_q_norm[j], mla_kv_norm[j], mla_w_q_up[j], mla_w_kv_up[j], mla_w_out[j])
        else:
            mix = hgrn2_mixer(h, hg_w_in[j], lb_all[layer], hg_norm[j], hg_w_out[j])
        h = layer_norm(DN_ALPHA * h + mix, ln_mix_g[layer], ln_mix_b[layer])
        ffn = peer_ffn(h, peer_w_q[layer], peer_sub_keys[layer], peer_u[layer], peer_v[layer])
        h = layer_norm(DN_ALPHA * h + ffn, ln_ffn_g[layer], ln_ffn_b[layer])
    return h


_drawn_inputs = setup_inputs


def setup_inputs(seed=0):
    import zlib

    import numpy as np

    out = dict(_drawn_inputs(seed))
    spreads = {}
    factors = {'na_rel_bias': 5.534,
     'mla_q_norm': 8.0,
     'mla_kv_norm': 8.0,
     'ln_mix_g': 3.257,
     'ln_mix_b': 3.187,
     'ln_ffn_g': 3.67,
     'ln_ffn_b': 3.413}
    for name, (base, spread) in spreads.items():
        noise = np.random.default_rng([zlib.crc32(name.encode()), seed]).standard_normal(out[name].shape)
        drawn = base * np.exp(spread * noise) if base else spread * noise
        out[name] = __import__('jax').numpy.asarray(drawn.astype(out[name].dtype))
    for name, factor in factors.items():
        out[name] = (out[name] * factor).astype(out[name].dtype)
    return out
```

```python
import concourse.bass as bass
from concourse import mybir
from contextlib import ExitStack

P = 128
D = 1024
TOK = 256
TILES = TOK // P
DK = D // P
LAYERS = 2
ALPHA = (2.0 * LAYERS) ** 0.25
EPS = 1e-5

GRID_W = 64
ROWS = TOK // GRID_W
NA_KH, NA_KW = 8, 16
HEADS = 16
PAIRS = HEADS // 2
HD = 64
PAIR = 2 * HD
NA_SCALE = HD ** -0.5
BIAS_W = 2 * NA_KW - 1
BIAS_H = 2 * NA_KH - 1

RANK = 256
RK = RANK // P
ROPE = 32
QW = HD + ROPE
KVW = 2 * HD
MLA_SCALE = QW ** -0.5

PH = 8
KEYS = 128
DKEY = 128
EXPERTS = KEYS * KEYS
TOPK = 16
GROUPS = TILES * PH
RING = 8
NEG = -1e30


def program(nc, x, na_w_in, rel_bias, na_w_out, mla_w_in, mla_q_norm, mla_kv_norm, w_q_up, w_kv_up,
            mla_w_out, peer_w_q, sub_keys, peer_u, peer_v, ln_mix_g, ln_mix_b, ln_ffn_g, ln_ffn_b,
            rope_cos, rope_sin, out):
    f32 = mybir.dt.float32
    i32 = mybir.dt.int32
    u32 = mybir.dt.uint32
    ALU = mybir.AluOpType
    ACT = mybir.ActivationFunctionType
    X = mybir.AxisListType.X
    ds = bass.ds

    with ExitStack() as ctx:
        def sb(name, shape, dt=f32):
            return ctx.enter_context(nc.sbuf_tensor(name, shape, dt))

        def bank(name):
            return ctx.enter_context(nc.psum_tensor(name, [P, 512], f32))

        def sem(name):
            return ctx.enter_context(nc.semaphore(name))

        ident = sb("ident", [P, P])
        alpha_ident = sb("alpha_ident", [P, P])
        iota16 = sb("iota16", [P, TOPK])
        na_mask = sb("na_mask", [P, GRID_W])
        eps_col = sb("eps_col", [P, 1])
        keys = sb("keys", [P, LAYERS * 2, DKEY])
        keysT = sb("keysT", [P, LAYERS * 2, KEYS])
        g_col = sb("g_col", [P, 3, DK])
        b_col = sb("b_col", [P, 3, DK])
        norm_col = sb("norm_col", [P, 2 * RK])
        cos_t = sb("cos_t", [2 * ROPE, TOK])
        sin_t = sb("sin_t", [2 * ROPE, TOK])
        nat = sb("nat", [P, TILES, D])
        hT = sb("hT", [P, DK, TOK])
        xhat = sb("xhat", [P, D])
        g_row = sb("g_row", [P, D])
        b_row = sb("b_row", [P, D])
        ln_stats = sb("ln_stats", [P, 2, 6])
        ln_mv = sb("ln_mv", [P, 2])
        ln_std = sb("ln_std", [P, 1])
        ln_rstd = sb("ln_rstd", [P, 1])
        w_qk = sb("w_qk", [P, 2, DK, PAIR])
        w_v = sb("w_v", [P, DK, PAIR])
        w_o = sb("w_o", [P, D])
        shared = sb("shared", [P, 2, TILES, 2, ROWS, GRID_W])
        bias_raw = shared[:, 0, :, :, :, :]
        bias = shared[:, 1, :, :, :, :]
        w_lat = sb("w_lat", [P, DK, 2 * RANK + ROPE])
        w_kpe = sb("w_kpe", [P, DK, 2, 2, ROPE])
        w_qn = sb("w_qn", [P, RK, 2, HD])
        w_qr = sb("w_qr", [P, RK, 2, ROPE])
        w_qsw = sb("w_qsw", [P, RK, 2, ROPE])
        w_kn = sb("w_kn", [P, RK, 2, HD])
        w_vu = sb("w_vu", [P, RK, 2, HD])
        cn = sb("cn", [P, 2 * RK, P])
        cT = sb("cT", [P, 2 * RK, TOK])
        sq_junk = sb("sq_junk", [P, 2, RANK])
        c_ss = sb("c_ss", [P, 2])
        c_ms = sb("c_ms", [P, 2])
        c_std = sb("c_std", [P, 2])
        c_rstd = sb("c_rstd", [P, 2])
        kpe = sb("kpe", [2 * ROPE, TOK])
        qpe = sb("qpe", [2 * ROPE, TOK])
        rope_a = sb("rope_a", [2 * ROPE, TOK])
        rope_b = sb("rope_b", [2 * ROPE, TOK])
        qk = sb("qk", [P, 2, TOK])
        v_sb = sb("v_sb", [P, TILES, PAIR])
        logits = [sb(f"logits{i}", [P, TILES, TOK]) for i in range(2)]
        probs = [sb(f"probs{i}", [P, TILES, TOK]) for i in range(2)]
        probsT = [sb(f"probsT{i}", [P, TILES, TOK]) for i in range(2)]
        nmax = sb("nmax", [P, 2, TILES])
        psum_row = sb("psum_row", [P, 2, TILES])
        rsum = sb("rsum", [P, 2, TILES])
        oT = sb("oT", [P, TOK])
        w_pq = sb("w_pq", [P, DK, 2 * DKEY])
        qT = sb("qT", [P, 2, TOK])
        key_top = sb("key_top", [P, TILES, 2, TOPK])
        key_idx = sb("key_idx", [P, TILES, 2, TOPK], u32)
        key_idxf = sb("key_idxf", [P, TILES, 2, TOPK])
        key_left = sb("key_left", [P, TILES, 2, KEYS])
        cand = sb("cand", [P, TILES, TOPK, TOPK])
        cand_left = sb("cand_left", [P, TILES, TOPK * TOPK])
        best = sb("best", [P, TILES, TOPK])
        pos = sb("pos", [P, TILES, TOPK], u32)
        pos_a = sb("pos_a", [P, TILES, TOPK], u32)
        pos_b = sb("pos_b", [P, TILES, TOPK], u32)
        pos_af = sb("pos_af", [P, TILES, TOPK])
        pos_bf = sb("pos_bf", [P, TILES, TOPK])
        hit = sb("hit", [P, TILES * TOPK, TOPK])
        pick_a = sb("pick_a", [P, TILES, TOPK])
        pick_b = sb("pick_b", [P, TILES, TOPK])
        best_d = sb("best_d", [P, TILES, TOPK])
        best_e = sb("best_e", [P, TILES, TOPK])
        gate_s = sb("gate_s", [P, TILES])
        gate_r = sb("gate_r", [P, TILES])
        gate = sb("gate", [P, TILES, PH * TOPK])
        expert = sb("expert", [P, TILES, PH * TOPK], i32)
        idx_u = sb("idx_u", [P, 2, RING], i32)
        idx_v = sb("idx_v", [P, 2, RING], i32)
        u_rows = sb("u_rows", [P, RING, D])
        v_rows = sb("v_rows", [P, RING, D])
        hid = sb("hid", [P, TOPK])
        act_hid = sb("act_hid", [P, TOPK])
        wts = sb("wts", [P, TOPK])
        diag = shared[:, :, :, :, :, :].rearrange("p a t i r c -> p (a t i r c)").rearrange("p (k n) -> p k n", k=TOPK)
        y01 = ctx.enter_context(nc.psum_tensor("y01", [P, TILES, 2, 512], f32))
        b_qk = bank("b_qk")
        b_vo = bank("b_vo")
        att = ctx.enter_context(nc.psum_tensor("att", [P, 2, 512], f32))
        b_att = [att[:, i, :] for i in range(2)]
        px = y01[:, 0, :, :]
        ffn = [y01[:, 1, :, :], att[:, :, :]]
        v_ps = b_vo[:, 0:TILES * PAIR].rearrange("p (t n) -> p t n", t=TILES)
        oT_ps = b_vo[:, TILES * PAIR:]
        qk_ps = b_qk[:, :].rearrange("p (s n) -> p s n", s=2)
        scores_ps = b_vo[:, :].rearrange("p (t c n) -> p t c n", t=TILES, c=2)

        s_x = sem("x_loaded"); s_small = sem("small_loaded"); s_lat = sem("w_lat_loaded")
        s_wqk = sem("w_qk_loaded"); s_wv = sem("w_v_loaded"); s_wo = sem("w_o_loaded")
        s_wqu = sem("w_qu_loaded"); s_wqr = sem("w_q_rope_loaded"); s_wkvu = sem("w_kvu_loaded"); s_braw = sem("bias_raw_loaded")
        s_rows = sem("ln_rows_loaded"); s_wpq = sem("w_pq_loaded"); s_out = sem("out_stored")
        s_const = sem("constants_made"); s_bias = sem("bias_masked"); s_swap = sem("rope_cols_swapped")
        s_xtr = sem("x_transposed_ps"); s_xT = sem("x_transposed_sb"); s_ktr = sem("keysT_ps"); s_kT = sem("keysT_sb")
        s_qkps = sem("qk_in_psum"); s_qksb = sem("qk_in_sbuf")
        s_vps = sem("v_in_psum"); s_vsb = sem("v_in_sbuf")
        s_sc = sem("logits_in_psum"); s_max = sem("row_max_ready"); s_exp = sem("exp_done")
        s_prob = sem("probs_ready"); s_ptps = sem("probsT_in_psum"); s_ptsb = sem("probsT_in_sbuf")
        s_pv = sem("pv_in_psum"); s_oT = sem("oT_in_sbuf"); s_y = sem("out_product_done")
        s_badd = sem("bias_added")
        s_peps = sem("q_rope_in_psum"); s_pesb = sem("q_rope_done")
        s_cps = sem("latents_in_psum"); s_css = sem("latent_squares"); s_cms = sem("latent_ms")
        s_cstd = sem("latent_std"); s_cn = sem("latents_normed"); s_ctr = sem("latentsT_in_psum")
        s_cT = sem("latentsT_in_sbuf"); s_kpps = sem("k_rope_in_psum"); s_kpsb = sem("k_rope_done")
        s_var = sem("ln_var_ready"); s_std = sem("ln_std_ready"); s_xhat = sem("ln_xhat_ready")
        s_tr = sem("ln_transposed_ps"); s_hT = sem("ln_hT_ready"); s_nat = sem("ln_nat_ready")
        s_px = sem("px_ready")
        s_qTps = sem("peer_q_in_psum"); s_qTsb = sem("peer_q_in_sbuf"); s_ks = sem("key_scores_ready")
        s_bd = sem("best_minus_max"); s_be = sem("best_exp"); s_top = sem("experts_chosen")
        s_ix = sem("indices_copied")
        s_ug = [sem(f"u_rows_landed{i}") for i in range(RING)]
        s_vg = [sem(f"v_rows_landed{i}") for i in range(RING)]
        s_dot = sem("dot_done"); s_gelu = sem("gelu_done"); s_wts = sem("weights_ready")
        s_diag = sem("diag_ready"); s_acc = sem("v_accumulated"); s_pool = sem("pool_step"); s_dstep = sem("dve_step")

        block = ctx.enter_context(nc.Block())

        def norm_no(layer, ffn_norm, tile):
            return 4 * layer + 2 * ffn_norm + tile

        def rows_reversed(ap):
            return bass.AP(ap.tensor, ap.offset + GRID_W - 1, [list(ap.ap[0]), [GRID_W, ROWS], [-1, GRID_W]])

        def dots_done(n):
            return n + RING

        def products_done(n):
            return n + RING

        @block.sync
        def _(sp):
            for t in range(TILES):
                sp.dma_start(nat[:, t, :], x[0, t * P:(t + 1) * P, :]).then_inc(s_x, 16)

            w_in3 = na_w_in[0].rearrange("(k p) (s c) -> s p k c", p=P, s=3)

            def load_na_qk(j):
                for s in range(2):
                    sp.dma_start(w_qk[:, s, :, :], w_in3[s][:, :, ds(j * PAIR, PAIR)]).then_inc(s_wqk, 16)

            def load_na_v(j):
                sp.dma_start(w_v[:, :, :], w_in3[2][:, :, ds(j * PAIR, PAIR)]).then_inc(s_wv, 16)

            def load_out_rows(j, w):
                sp.dma_start(w_o[:, :], w[ds(j * PAIR, PAIR), :]).then_inc(s_wo, 16)

            def load_bias(j):
                for t in range(TILES):
                    for rho in range(2):
                        for i in range(2):
                            r = 2 * t + rho
                            first = (i * BIAS_H + NA_KH - 1 - r) * BIAS_W + NA_KW - GRID_W
                            src = bass.AP(rel_bias.tensor, j * (2 * BIAS_H * BIAS_W) + first,
                                          [[1, GRID_W], [BIAS_W, ROWS], [1, GRID_W]])
                            sp.dma_start(bias_raw[rho * GRID_W:(rho + 1) * GRID_W, t, i, :, :], src)\
                              .then_inc(s_braw, 16)

            load_na_qk(0)
            load_na_v(0)
            load_bias(0)
            sp.dma_start(keys[:, :, :], sub_keys.rearrange("l c n d -> n (l c) d")).then_inc(s_small, 16)
            for n, (g, b) in enumerate(((ln_mix_g[0], ln_mix_b[0]), (ln_ffn_g[0], ln_ffn_b[0]),
                                        (ln_mix_g[1], ln_mix_b[1]))):
                sp.dma_start(g_col[:, n, :], g.rearrange("(k p) -> p k", p=P),
                             allow_slow_non_contiguous=True).then_inc(s_small, 16)
                sp.dma_start(b_col[:, n, :], b.rearrange("(k p) -> p k", p=P),
                             allow_slow_non_contiguous=True).then_inc(s_small, 16)
            sp.dma_start(norm_col[:, 0:RK], mla_q_norm[0].rearrange("(k p) -> p k", p=P),
                         allow_slow_non_contiguous=True).then_inc(s_small, 16)
            sp.dma_start(norm_col[:, RK:], mla_kv_norm[0].rearrange("(k p) -> p k", p=P),
                         allow_slow_non_contiguous=True).then_inc(s_small, 16)
            sp.dma_start(cos_t[:, :], rope_cos).then_inc(s_small, 16)
            sp.dma_start(sin_t[:, :], rope_sin).then_inc(s_small, 16)

            def load_norm_rows(n, g, b):
                if n:
                    sp.wait_ge(s_nat, 2 * n)
                sp.dma_start(g_row[:, :], g.partition_broadcast(P)).then_inc(s_rows, 16)
                sp.dma_start(b_row[:, :], b.partition_broadcast(P)).then_inc(s_rows, 16)

            load_norm_rows(0, ln_mix_g[0:1, :], ln_mix_b[0:1, :])

            with sp.Fori(1, PAIRS) as j:
                sp.wait_ge(s_qkps, j)
                load_na_qk(j)
                sp.wait_ge(s_vps, j)
                load_na_v(j)
                sp.wait_ge(s_bias, j)
                load_bias(j)
                sp.wait_ge(s_sc, 2 * j)
                load_out_rows(j - 1, na_w_out[0])
            sp.wait_ge(s_sc, 2 * PAIRS)
            load_out_rows(PAIRS - 1, na_w_out[0])

            def load_pq(layer, h):
                sp.dma_start(w_pq[:, :, :], peer_w_q[layer].rearrange("(k p) n -> p k n", p=P)
                             [:, :, ds(h * 2 * DKEY, 2 * DKEY)]).then_inc(s_wpq, 16)

            def peer_loads(layer):
                with sp.Fori(1, PH) as h:
                    sp.wait_ge(s_qTps, layer * PH + h)
                    load_pq(layer, h)

            load_pq(0, 0)
            sp.dma_start(w_lat[:, :, :], mla_w_in[0].rearrange("(k p) n -> p k n", p=P)).then_inc(s_lat, 16)
            load_norm_rows(1, ln_ffn_g[0:1, :], ln_ffn_b[0:1, :])
            peer_loads(0)

            def load_mla_q(j):
                cols = w_q_up[0].rearrange("(k p) n -> p k n", p=P)
                for i in range(2):
                    sp.dma_start(w_qr[:, :, i, :], cols[:, :, ds(j * 2 * QW + i * QW + HD, ROPE)]).then_inc(s_wqr, 16)
                for i in range(2):
                    sp.dma_start(w_qn[:, :, i, :], cols[:, :, ds(j * 2 * QW + i * QW, HD)]).then_inc(s_wqu, 16)

            def load_mla_kv(j):
                cols = w_kv_up[0].rearrange("(k p) n -> p k n", p=P)
                for i in range(2):
                    for part, w in enumerate((w_kn, w_vu)):
                        sp.dma_start(w[:, :, i, :], cols[:, :, ds(j * 2 * KVW + i * KVW + part * HD, HD)])\
                          .then_inc(s_wkvu, 16)

            load_mla_q(0)
            load_mla_kv(0)
            sp.wait_ge(s_qTps, PH)
            load_pq(1, 0)
            load_norm_rows(2, ln_mix_g[1:2, :], ln_mix_b[1:2, :])
            with sp.Fori(1, PAIRS) as j:
                sp.wait_ge(s_qkps, PAIRS + j)
                load_mla_q(j)
                sp.wait_ge(s_vps, PAIRS + j)
                load_mla_kv(j)
                sp.wait_ge(s_sc, 2 * (PAIRS + j))
                load_out_rows(j - 1, mla_w_out[0])
            sp.wait_ge(s_sc, 2 * (2 * PAIRS))
            load_out_rows(PAIRS - 1, mla_w_out[0])
            load_norm_rows(3, ln_ffn_g[1:2, :], ln_ffn_b[1:2, :])
            peer_loads(1)
            for t in range(TILES):
                sp.wait_ge(s_nat, norm_no(1, 1, t) + 1)
                sp.dma_start(out[0, t * P:(t + 1) * P, :], nat[:, t, :]).then_inc(s_out, 16)
            sp.wait_ge(s_out, 16 * TILES)

        @block.gpsimd
        def _(pool):
            pool.memset(ident[:, :], 0.0).then_inc(s_pool, 1)
            pool.memset(alpha_ident[:, :], 0.0).then_inc(s_pool, 1)
            pool.memset(na_mask[:, :], 0.0).then_inc(s_pool, 1)
            pool.memset(eps_col[:, :], EPS).then_inc(s_const, 1)
            pool.iota(iota16[:, :], [[1, TOPK]], base=0, channel_multiplier=0,
                      allow_small_or_imprecise_dtypes=True).then_inc(s_const, 1)
            pool.wait_ge(s_pool, 3)
            pool.affine_select(out=ident[:, :], in_=ident[:, :], compare_op=ALU.not_equal, fill=1.0,
                               base=0, pattern=[[-1, P]], channel_multiplier=1).then_inc(s_const, 1)
            pool.affine_select(out=alpha_ident[:, :], in_=alpha_ident[:, :], compare_op=ALU.not_equal,
                               fill=ALPHA, base=0, pattern=[[-1, P]], channel_multiplier=1).then_inc(s_const, 1)
            pool.wait_ge(s_const, 4)
            half, edge = NA_KW // 2, GRID_W - NA_KW
            for rho in range(2):
                left = na_mask[rho * GRID_W:(rho + 1) * GRID_W, 0:edge]
                pool.affine_select(out=left, in_=left, compare_op=ALU.is_ge, fill=NEG,
                                   base=half - (GRID_W - 1), pattern=[[1, edge]], channel_multiplier=1)\
                    .then_inc(s_pool, 1)
                pool.wait_ge(s_pool, 4 + 2 * rho)
                right = na_mask[rho * GRID_W:(rho + 1) * GRID_W, NA_KW:GRID_W]
                pool.affine_select(out=right, in_=right, compare_op=ALU.is_ge, fill=NEG,
                                   base=half - 1 - NA_KW + GRID_W - 1, pattern=[[-1, edge]],
                                   channel_multiplier=-1).then_inc(s_pool, 1)
                pool.wait_ge(s_pool, 5 + 2 * rho)

            rows = TILES * 2 * ROWS
            mask_b = na_mask[:, :].unsqueeze(1).broadcast_to([P, rows, GRID_W])

            def mask_bias(j, first=False):
                pool.wait_ge(s_braw, 128 * (j + 1))
                if not first:
                    pool.wait_ge(s_badd, 2 * j)
                nc.gpsimd.tensor_tensor(bias.rearrange("p t i r c -> p (t i r) c"),
                                        bias_raw.rearrange("p t i r c -> p (t i r) c"),
                                        mask_b, ALU.add).then_inc(s_bias, 1)

            mask_bias(0, True)
            with pool.Fori(1, PAIRS) as j:
                mask_bias(j)

            expert_flat = expert[:, :, :].rearrange("p t n -> p (t n)")

            def copy_indices(dst, half_no, group):
                nc.gpsimd.tensor_copy(dst[:, half_no, :],
                                      expert_flat[:, ds(group * TOPK + half_no * RING, RING)]).then_inc(s_ix, 1)

            u_table = peer_u.rearrange("l e d -> (l e) d")
            v_table = peer_v.rearrange("l e d -> (l e) d")

            def gather_group(layer, g, copies, heads=None, with_u=True, with_v=True):
                base = layer * GROUPS * TOPK
                if heads is not None:
                    pool.wait_ge(s_top, layer * PH + heads)
                    pool.sem_inc(s_pool, 1)
                for half_no in range(2):
                    if with_u:
                        copy_indices(idx_u, half_no, g)
                        copies = copies + 1
                    if with_v:
                        copy_indices(idx_v, half_no, g - 1)
                        copies = copies + 1
                    pool.wait_ge(s_ix, copies)
                    pool.sem_inc(s_pool, 1)
                    for b in range(RING):
                        k = half_no * RING + b
                        if with_u:
                            pool.wait_ge(s_dot, dots_done(base + g * TOPK + k + 1 - RING))
                            pool.sem_inc(s_pool, 1)
                            pool.indirect_dma_start(u_rows[:, b, :], None, u_table,
                                                    bass.IndirectOffsetOnAxis(ap=idx_u[:, half_no, b:b + 1], axis=0))\
                                .then_inc(s_ug[b], 16)
                        if with_v:
                            pool.wait_ge(s_acc, products_done(base + (g - 1) * TOPK + k + 1 - RING))
                            pool.sem_inc(s_pool, 1)
                            pool.indirect_dma_start(v_rows[:, b, :], None, v_table,
                                                    bass.IndirectOffsetOnAxis(ap=idx_v[:, half_no, b:b + 1], axis=0))\
                                .then_inc(s_vg[b], 16)

            def gathers(layer):
                start = layer * GROUPS * 4
                gather_group(layer, 0, start, heads=1, with_v=False)
                with pool.Fori(1, PH) as g:
                    gather_group(layer, g, start + 4 * g - 2, heads=g + 1)
                with pool.Fori(PH, GROUPS) as g:
                    gather_group(layer, g, start + 4 * g - 2)
                gather_group(layer, GROUPS, start + 4 * GROUPS - 2, with_u=False)

            gathers(0)

            hr = ROPE // 2
            pool.wait_ge(s_lat, 16)
            pool.sem_inc(s_pool, 1)
            for rep in range(2):
                nc.gpsimd.tensor_copy(w_kpe[:, :, 0, rep, :], w_lat[:, :, 2 * RANK:])
                for part in range(2):
                    src = 2 * RANK + (1 - part) * hr
                    last = nc.gpsimd.tensor_copy(w_kpe[:, :, 1, rep, part * hr:(part + 1) * hr],
                                                 w_lat[:, :, src:src + hr])
            last.then_inc(s_swap, 1)

            def swap_q_rope(j, first=False):
                pool.wait_ge(s_wqr, 32 * (j + 1))
                pool.sem_inc(s_pool, 1)
                if not first:
                    pool.wait_ge(s_peps, j)
                    pool.sem_inc(s_pool, 1)
                for part in range(2):
                    src = (1 - part) * hr
                    last = nc.gpsimd.tensor_copy(w_qsw[:, :, :, part * hr:(part + 1) * hr],
                                                 w_qr[:, :, :, src:src + hr])
                last.then_inc(s_swap, 1)

            swap_q_rope(0, True)
            with pool.Fori(1, PAIRS) as j:
                swap_q_rope(j)
            gathers(1)

        @block.tensor
        def _(pe):
            pe.sem_inc(s_acc, RING)
            pe.wait_ge(s_const, 4)
            pe.wait_ge(s_x, 16 * TILES)
            for t in range(TILES):
                for half in range(2):
                    n = 2 * t + half
                    if n >= 2:
                        pe.wait_ge(s_xT, n - 1)
                    for c in range(4):
                        k = 4 * half + c
                        last = nc.tensor.transpose(b_att[n % 2][:, c * P:(c + 1) * P],
                                                   nat[:, t, k * P:(k + 1) * P], ident[:, :])
                    last.then_inc(s_xtr, 1)
            pe.wait_ge(s_small, 16 * 11)
            for n in range(LAYERS * 2):
                last = nc.tensor.transpose(b_qk[:, n * P:(n + 1) * P], keys[:, n, :], ident[:, :])
            last.then_inc(s_ktr, 1)

            def seed(acc, t, done=None):
                for c in range(2):
                    last = nc.tensor.matmul(acc[:, c, :], alpha_ident[:, :], nat[:, t, c * 512:(c + 1) * 512],
                                            start=True, stop=False)
                return last

            def scores_na(j, i):
                for t in range(TILES):
                    last = nc.tensor.matmul(b_att[i][:, t * TOK:(t + 1) * TOK],
                                            qk[i * HD:(i + 1) * HD, 0, t * P:(t + 1) * P],
                                            qk[i * HD:(i + 1) * HD, 1, :], start=True, stop=True)
                last.then_inc(s_sc, 1)

            def scores_mla(j, i):
                for t in range(TILES):
                    nc.tensor.matmul(b_att[i][:, t * TOK:(t + 1) * TOK],
                                     qk[i * HD:(i + 1) * HD, 0, t * P:(t + 1) * P],
                                     qk[i * HD:(i + 1) * HD, 1, :], start=True, stop=False)
                    last = nc.tensor.matmul(b_att[i][:, t * TOK:(t + 1) * TOK],
                                            qpe[i * ROPE:(i + 1) * ROPE, t * P:(t + 1) * P],
                                            kpe[i * ROPE:(i + 1) * ROPE, :], start=False, stop=True)
                last.then_inc(s_sc, 1)

            def transpose_probs(jj, i):
                pe.wait_ge(s_prob, 2 * jj + i + 1)
                for t in range(TILES):
                    for kt in range(TILES):
                        last = nc.tensor.transpose(b_att[i][:, kt * TOK + t * P:kt * TOK + (t + 1) * P],
                                                   probs[i][:, t, kt * P:(kt + 1) * P], ident[:, :])
                last.then_inc(s_ptps, 1)

            def pv(jj, i):
                pe.wait_ge(s_ptsb, 2 * jj + i + 1)
                for kt in range(TILES):
                    last = nc.tensor.matmul(oT_ps[i * HD:(i + 1) * HD, :], v_sb[:, kt, i * HD:(i + 1) * HD],
                                            probsT[i][:, kt, :], start=(kt == 0), stop=(kt == TILES - 1))
                last.then_inc(s_pv, 1)

            def out_product(jj, last_pair):
                pe.wait_ge(s_wo, 16 * (jj + 1))
                pe.wait_ge(s_oT, jj + 1)
                for t in range(TILES):
                    for c in range(2):
                        last = nc.tensor.matmul(y01[:, t, c, :], oT[:, t * P:(t + 1) * P],
                                                w_o[:, c * 512:(c + 1) * 512], start=False, stop=last_pair)
                last.then_inc(s_y, 1)

            def project_qk_na(j):
                pe.wait_ge(s_wqk, 32 * (j + 1))
                for s in range(2):
                    for k in range(DK):
                        last = nc.tensor.matmul(qk_ps[:, s, :], w_qk[:, s, k, :], hT[:, k, :],
                                                start=(k == 0), stop=(k == DK - 1))
                last.then_inc(s_qkps, 1)

            def project_v_na(j):
                pe.wait_ge(s_wv, 16 * (j + 1))
                for t in range(TILES):
                    for k in range(DK):
                        last = nc.tensor.matmul(v_ps[:, t, :], hT[:, k, t * P:(t + 1) * P], w_v[:, k, :],
                                                start=(k == 0), stop=(k == DK - 1))
                last.then_inc(s_vps, 1)

            def pair_na(j, last_pair=False):
                pe.wait_ge(s_qksb, j + 1)
                for i in range(2):
                    scores_na(j, i)
                if not last_pair:
                    project_qk_na(j + 1)
                pe.wait_ge(s_vsb, j + 1)
                for i in range(2):
                    transpose_probs(j, i)
                for i in range(2):
                    pv(j, i)
                out_product(j, last_pair)
                if not last_pair:
                    project_v_na(j + 1)

            for t in range(TILES):
                seed(y01[:, t, :, :], t)
            pe.wait_ge(s_xT, 4)
            pe.wait_ge(s_kT, 1)
            project_qk_na(0)
            project_v_na(0)
            with pe.Fori(0, PAIRS - 1) as j:
                pair_na(j)
            pair_na(PAIRS - 1, True)

            def norm_transposes(n, banks):
                pe.wait_ge(s_xhat, n + 1)
                for half in range(2):
                    for c in range(4):
                        k = 4 * half + c
                        last = nc.tensor.transpose(banks[half][:, c * P:(c + 1) * P],
                                                   xhat[:, k * P:(k + 1) * P], ident[:, :])
                    last.then_inc(s_tr, 1)

            def peer_queries(layer, h):
                pe.wait_ge(s_wpq, 16 * (layer * PH + h + 1))
                for c in range(2):
                    for k in range(DK):
                        last = nc.tensor.matmul(qk_ps[:, c, :], w_pq[:, k, c * DKEY:(c + 1) * DKEY],
                                                hT[:, k, :], start=(k == 0), stop=(k == DK - 1))
                last.then_inc(s_qTps, 1)

            def key_scores(layer, h, first=False):
                pe.wait_ge(s_qTsb, layer * PH + h + 1)
                if not first:
                    pe.wait_ge(s_top, layer * PH + h)
                for t in range(TILES):
                    for c in range(2):
                        last = nc.tensor.matmul(scores_ps[:, t, c, :], qT[:, c, t * P:(t + 1) * P],
                                                keysT[:, 2 * layer + c, :], start=True, stop=True)
                last.then_inc(s_ks, 1)

            def add_experts(layer, tile, g, stop=False):
                base = layer * GROUPS
                for k in range(TOPK):
                    b = k % RING
                    pe.wait_ge(s_diag, (base + g) * TOPK + k + 1)
                    pe.wait_ge(s_vg[b], 16 * ((base + g) * 2 + k // RING + 1))
                    for c in range(2):
                        last = nc.tensor.matmul(ffn[tile][:, c, :], diag[:, k, :],
                                                v_rows[:, b, c * 512:(c + 1) * 512],
                                                start=False, stop=stop and k == TOPK - 1)
                    last.then_inc(s_acc, 1)

            def peer(layer):
                mix = norm_no(layer, 0, 0)
                norm_transposes(mix, b_att)
                pe.wait_ge(s_hT, 2 * norm_no(layer, 0, 0) + 2)
                norm_transposes(mix + 1, b_att)
                pe.wait_ge(s_hT, 2 * norm_no(layer, 0, 1) + 2)
                peer_queries(layer, 0)
                key_scores(layer, 0, first=layer == 0)
                pe.wait_ge(s_nat, mix + 2)
                for t in range(TILES):
                    seed(ffn[t], t)
                peer_queries(layer, 1)
                key_scores(layer, 1)
                with pe.Fori(1, PH - 1) as g:
                    peer_queries(layer, g + 1)
                    key_scores(layer, g + 1)
                    add_experts(layer, 0, g - 1)
                add_experts(layer, 0, PH - 2)
                add_experts(layer, 0, PH - 1, stop=True)
                if layer == 0:
                    norm_transposes(norm_no(layer, 1, 0), (b_qk[:, :], b_vo[:, :]))
                with pe.Fori(PH + 1, GROUPS) as g:
                    add_experts(layer, 1, g - 1)
                add_experts(layer, 1, GROUPS - 1, stop=True)
                if layer == 0:
                    pe.wait_ge(s_hT, 2 * norm_no(layer, 1, 0) + 2)
                    norm_transposes(norm_no(layer, 1, 1), (b_qk[:, :], b_vo[:, :]))

            peer(0)

            pe.wait_ge(s_nat, norm_no(0, 1, 1) + 1)
            for t in range(TILES):
                seed(y01[:, t, :, :], t)
            pe.wait_ge(s_hT, 2 * norm_no(0, 1, 1) + 2)
            for t in range(TILES):
                for k in range(DK):
                    last = nc.tensor.matmul(b_att[t], hT[:, k, t * P:(t + 1) * P], w_lat[:, k, 0:2 * RANK],
                                            start=(k == 0), stop=(k == DK - 1))
                last.then_inc(s_cps, 1)
            pe.wait_ge(s_swap, 1)
            for s in range(2):
                for k in range(DK):
                    last = nc.tensor.matmul(qk_ps[0:2 * ROPE, s, :],
                                            w_kpe[:, k, s, :, :].rearrange("p r c -> p (r c)"), hT[:, k, :],
                                            start=(k == 0), stop=(k == DK - 1))
            last.then_inc(s_kpps, 1)
            for t in range(TILES):
                pe.wait_ge(s_cn, t + 1)
                for c in range(2 * RK):
                    last = nc.tensor.transpose(b_vo[:, c * P:(c + 1) * P] if t == 0 else
                                               b_att[0][:, c * P:(c + 1) * P], cn[:, c, :], ident[:, :])
                last.then_inc(s_ctr, 1)

            def project_qpe(j):
                pe.wait_ge(s_wqr, 32 * (j + 1))
                pe.wait_ge(s_swap, j + 2)
                for s in range(2):
                    for k in range(RK):
                        w = w_qr if s == 0 else w_qsw
                        last = nc.tensor.matmul(qk_ps[0:2 * ROPE, s, :],
                                                w[:, k, :, :].rearrange("p h n -> p (h n)"), cT[:, k, :],
                                                start=(k == 0), stop=(k == RK - 1))
                last.then_inc(s_peps, 1)

            def project_qk_mla(j):
                pe.wait_ge(s_wqu, 32 * (j + 1))
                pe.wait_ge(s_wkvu, 64 * (j + 1))
                pe.wait_ge(s_pesb, j + 1)
                for s, w in ((0, w_qn), (1, w_kn)):
                    for k in range(RK):
                        last = nc.tensor.matmul(qk_ps[:, s, :], w[:, k, :, :].rearrange("p h n -> p (h n)"), cT[:, RK * s + k, :],
                                                start=(k == 0), stop=(k == RK - 1))
                last.then_inc(s_qkps, 1)

            def project_v_mla(j):
                for t in range(TILES):
                    for k in range(RK):
                        last = nc.tensor.matmul(v_ps[:, t, :], cT[:, RK + k, t * P:(t + 1) * P],
                                                w_vu[:, k, :, :].rearrange("p h n -> p (h n)"), start=(k == 0), stop=(k == RK - 1))
                last.then_inc(s_vps, 1)

            def pair_mla(j, last_pair=False):
                jj = PAIRS + j
                pe.wait_ge(s_qksb, jj + 1)
                for i in range(2):
                    scores_mla(j, i)
                if not last_pair:
                    project_qpe(j + 1)
                pe.wait_ge(s_vsb, jj + 1)
                transpose_probs(jj, 0)
                if not last_pair:
                    project_qk_mla(j + 1)
                transpose_probs(jj, 1)
                for i in range(2):
                    pv(jj, i)
                out_product(jj, last_pair)
                if not last_pair:
                    project_v_mla(j + 1)

            pe.wait_ge(s_cT, TILES)
            pe.wait_ge(s_kpsb, 1)
            project_qpe(0)
            project_qk_mla(0)
            project_v_mla(0)
            with pe.Fori(0, PAIRS - 1) as j:
                pair_mla(j)
            pair_mla(PAIRS - 1, True)
            peer(1)

        @block.scalar
        def _(act):
            for n in range(4):
                t, half = n // 2, n % 2
                act.wait_ge(s_xtr, n + 1)
                nc.scalar.activation(hT[:, 4 * half:4 * half + 4, t * P:(t + 1) * P],
                                     b_att[n % 2].rearrange("p (c n) -> p c n", c=4), ACT.Copy)\
                  .then_inc(s_xT, 1)
            act.wait_ge(s_ktr, 1)
            nc.scalar.activation(keysT[:, :, :], b_qk[:, :].rearrange("p (c n) -> p c n", c=2 * LAYERS),
                                 ACT.Copy).then_inc(s_kT, 1)

            def store_qk(jj, na):
                act.wait_ge(s_qkps, jj + 1)
                if na:
                    nc.scalar.activation(qk[:, 0, :].rearrange("p (r c) -> p r c", r=ROWS),
                                         rows_reversed(qk_ps[:, 0, :]), ACT.Copy, scale=NA_SCALE)
                else:
                    nc.scalar.activation(qk[:, 0, :], qk_ps[:, 0, :], ACT.Copy, scale=MLA_SCALE)
                nc.scalar.activation(qk[:, 1, :], qk_ps[:, 1, :], ACT.Copy).then_inc(s_qksb, 1)

            def store_v(jj):
                act.wait_ge(s_vps, jj + 1)
                nc.scalar.activation(v_sb[:, :, :], v_ps, ACT.Copy).then_inc(s_vsb, 1)

            def exps(jj, i, src):
                act.wait_ge(s_max, 2 * jj + i + 1)
                for t in range(TILES):
                    last = nc.scalar.activation(probs[i][:, t, :], src[:, t, :], ACT.Exp,
                                                bias=nmax[:, i, t:t + 1], accum_out=psum_row[:, i, t:t + 1])
                last.then_inc(s_exp, 1)

            def store_oT(jj, na):
                act.wait_ge(s_pv, 2 * jj + 2)
                if na:
                    nc.scalar.activation(oT[:, :].rearrange("p (r c) -> p r c", r=ROWS),
                                         rows_reversed(oT_ps), ACT.Copy).then_inc(s_oT, 1)
                else:
                    nc.scalar.activation(oT[:, :], oT_ps, ACT.Copy).then_inc(s_oT, 1)

            def pair(jj, src, na, last_pair=False):
                for i in range(2):
                    exps(jj, i, src[i])
                if not last_pair:
                    store_qk(jj + 1, na)
                store_oT(jj, na)
                if not last_pair:
                    store_v(jj + 1)

            def mixer(first, src, na):
                store_qk(first, na)
                store_v(first)
                with act.Fori(first, first + PAIRS - 1) as jj:
                    pair(jj, src, na)
                pair(first + PAIRS - 1, src, na, True)

            mixer(0, [logits[i][:, :, :] for i in range(2)], True)

            def norm(n, cols, banks, t):
                act.wait_ge(s_var, n + 1)
                nc.scalar.activation(ln_std[:, :], ln_mv[:, 1:2], ACT.Sqrt, bias=eps_col[:, :]).then_inc(s_std, 1)
                if cols is None:
                    return
                for half in range(2):
                    act.wait_ge(s_tr, 2 * n + half + 1)
                    for c in range(4):
                        k = 4 * half + c
                        last = nc.scalar.activation(hT[:, k, t * P:(t + 1) * P], banks[half][:, c * P:(c + 1) * P],
                                                    ACT.Identity, scale=g_col[:, cols, k:k + 1],
                                                    bias=b_col[:, cols, k:k + 1])
                    last.then_inc(s_hT, 1)

            def store_queries(layer, h):
                act.wait_ge(s_qTps, layer * PH + h + 1)
                nc.scalar.activation(qT[:, :, :], qk_ps, ACT.Copy).then_inc(s_qTsb, 1)

            def gate_exp(layer, h):
                act.wait_ge(s_bd, layer * PH + h + 1)
                nc.scalar.activation(best_e[:, :, :], best_d[:, :, :], ACT.Exp).then_inc(s_be, 1)

            def weigh(layer, g, first=False):
                base = layer * GROUPS
                act.wait_ge(s_dot, dots_done((base + g + 1) * TOPK))
                nc.scalar.activation(act_hid[:, :], hid[:, :], ACT.Gelu).then_inc(s_gelu, 1)
                act.wait_ge(s_wts, base + g + 1)
                for k in range(TOPK):
                    if not first:
                        act.wait_ge(s_acc, products_done((base + g - 1) * TOPK + k + 1))
                    nc.scalar.activation(diag[:, k, :], ident[:, :], ACT.Copy, scale=wts[:, k:k + 1])\
                      .then_inc(s_diag, 1)

            def peer(layer):
                n = norm_no(layer, 0, 0)
                for t in range(TILES):
                    norm(n + t, 2 * layer, b_att, t)
                store_queries(layer, 0)
                gate_exp(layer, 0)
                store_queries(layer, 1)
                gate_exp(layer, 1)
                weigh(layer, 0, first=layer == 0)
                with act.Fori(1, PH - 1) as g:
                    store_queries(layer, g + 1)
                    gate_exp(layer, g + 1)
                    weigh(layer, g)
                weigh(layer, PH - 1)
                weigh(layer, PH)
                norm(n + 2, 1 if layer == 0 else None, (b_qk[:, :], b_vo[:, :]), 0)
                with act.Fori(PH + 1, GROUPS) as g:
                    weigh(layer, g)
                norm(n + 3, 1 if layer == 0 else None, (b_qk[:, :], b_vo[:, :]), 1)

            peer(0)

            for t in range(TILES):
                act.wait_ge(s_cps, t + 1)
                for s in range(2):
                    last = nc.scalar.activation(sq_junk[:, s, :], b_att[t][:, s * RANK:(s + 1) * RANK], ACT.Square,
                                                accum_out=c_ss[:, s:s + 1])
                last.then_inc(s_css, 1)
                act.wait_ge(s_cms, t + 1)
                nc.scalar.activation(c_std[:, :], c_ms[:, :], ACT.Sqrt).then_inc(s_cstd, 1)
            mixer(PAIRS, [b_att[i].rearrange("p (t n) -> p t n", t=TILES) for i in range(2)], False)
            peer(1)

        @block.vector
        def _(dve):
            V = nc.vector
            dve.sem_inc(s_dot, RING)

            def softmax(jj, i, j=None, na=False):
                dve.wait_ge(s_sc, 2 * jj + i + 1)
                src = b_att[i].rearrange("p (t n) -> p t n", t=TILES)
                if na:
                    if i == 0:
                        dve.wait_ge(s_bias, jj + 1)
                    V.tensor_tensor(logits[i][:, :, :], src,
                                    bias[:, :, i, :, :].rearrange("p t r c -> p t (r c)"), ALU.add)\
                     .then_inc(s_badd, 1)
                    dve.drain()
                    src = logits[i][:, :, :]
                V.tensor_reduce(nmax[:, i, :], src, X, ALU.max, negate=True).then_inc(s_max, 1)

            def normalise(jj, i):
                dve.wait_ge(s_exp, 2 * jj + i + 1)
                V.reciprocal(rsum[:, i, :], psum_row[:, i, :])
                dve.drain()
                for t in range(TILES):
                    last = V.tensor_scalar(probs[i][:, t, :], probs[i][:, t, :], rsum[:, i, t:t + 1], None, ALU.mult)
                last.then_inc(s_prob, 1)

            def store_probsT(jj, i):
                dve.wait_ge(s_ptps, 2 * jj + i + 1)
                V.tensor_copy(probsT[i][:, :, :].rearrange("p t n -> p (t n)"), b_att[i]).then_inc(s_ptsb, 1)

            with dve.Fori(0, PAIRS) as j:
                for i in range(2):
                    softmax(j, i, na=True)
                for i in range(2):
                    normalise(j, i)
                for i in range(2):
                    store_probsT(j, i)

            def norm(n, src, t):
                for c in range(2):
                    V.bn_stats(ln_stats[:, c, :], src[:, c, :])
                dve.drain()
                V.bn_aggr(ln_mv[:, :], ln_stats[:, :, :].rearrange("p a b -> p (a b)")).then_inc(s_var, 1)
                dve.wait_ge(s_std, n + 1)
                V.reciprocal(ln_rstd[:, :], ln_std[:, :])
                dve.drain()
                if n and n < 7:
                    dve.wait_ge(s_tr, 2 * n)
                V.tensor_scalar(xhat[:, :].rearrange("p (c n) -> p c n", c=2), src,
                                ln_mv[:, 0:1], ln_rstd[:, 0:1], ALU.subtract, ALU.mult).then_inc(s_xhat, 1)
                dve.wait_ge(s_rows, 32 * (n // 2 + 1))
                dve.drain()
                V.tensor_tensor(nat[:, t, :], xhat[:, :], g_row[:, :], ALU.mult)
                dve.drain()
                V.tensor_tensor(nat[:, t, :], nat[:, t, :], b_row[:, :], ALU.add).then_inc(s_nat, 1)

            def key_top16(layer, h):
                dve.wait_ge(s_ks, layer * PH + h + 1)
                dve.sem_inc(s_dstep, 1)
                both = [(t, c) for t in range(TILES) for c in range(2)]
                for t, c in both:
                    V.max(key_top[:, t, c, 0:8], scores_ps[:, t, c, :])
                dve.drain()
                for t, c in both:
                    V.match_replace(key_left[:, t, c, :], key_top[:, t, c, 0:8], scores_ps[:, t, c, :], NEG)
                dve.drain()
                for t, c in both:
                    V.max(key_top[:, t, c, 8:16], key_left[:, t, c, :])
                for t, c in both:
                    V.max_index(key_idx[:, t, c, 0:8], key_top[:, t, c, 0:8], scores_ps[:, t, c, :])
                dve.drain()
                for t, c in both:
                    V.max_index(key_idx[:, t, c, 8:16], key_top[:, t, c, 8:16], key_left[:, t, c, :])
                dve.drain()
                V.tensor_copy(key_idxf[:, :, :, :], key_idx[:, :, :, :])

            def pair_top16():
                for t in range(TILES):
                    V.tensor_tensor(cand[:, t, :, :], key_top[:, t, 0, :].unsqueeze(2).broadcast_to([P, TOPK, TOPK]),
                                    key_top[:, t, 1, :].unsqueeze(1).broadcast_to([P, TOPK, TOPK]), ALU.add)
                flat = [cand[:, t, :, :].rearrange("p a b -> p (a b)") for t in range(TILES)]
                dve.drain()
                for t in range(TILES):
                    V.max(best[:, t, 0:8], flat[t])
                dve.drain()
                for t in range(TILES):
                    V.match_replace(cand_left[:, t, :], best[:, t, 0:8], flat[t], NEG)
                for t in range(TILES):
                    V.max_index(pos[:, t, 0:8], best[:, t, 0:8], flat[t])
                dve.drain()
                for t in range(TILES):
                    V.max(best[:, t, 8:16], cand_left[:, t, :])
                dve.drain()
                for t in range(TILES):
                    V.max_index(pos[:, t, 8:16], best[:, t, 8:16], cand_left[:, t, :])
                V.tensor_tensor(best_d[:, :, :], best[:, :, :], best[:, :, 0:1].broadcast_to([P, TILES, TOPK]),
                                ALU.subtract).then_inc(s_bd, 1)

            def expert_numbers(layer, h):
                dve.drain()
                V.tensor_scalar(pos_a[:, :, :], pos[:, :, :], 4, None, ALU.logical_shift_right)
                V.tensor_scalar(pos_b[:, :, :], pos[:, :, :], TOPK - 1, None, ALU.bitwise_and)
                dve.drain()
                V.tensor_copy(pos_af[:, :, :], pos_a[:, :, :])
                V.tensor_copy(pos_bf[:, :, :], pos_b[:, :, :])
                for c, (where, picked) in enumerate(((pos_af, pick_a), (pos_bf, pick_b))):
                    dve.drain()
                    V.tensor_tensor(hit[:, :, :],
                                    where[:, :, :].rearrange("p t k -> p (t k)").unsqueeze(2)
                                    .broadcast_to([P, TILES * TOPK, TOPK]),
                                    iota16[:, :].unsqueeze(1).broadcast_to([P, TILES * TOPK, TOPK]), ALU.is_equal)
                    dve.drain()
                    for t in range(TILES):
                        V.tensor_tensor(hit[:, t * TOPK:(t + 1) * TOPK, :], hit[:, t * TOPK:(t + 1) * TOPK, :],
                                        key_idxf[:, t, c, :].unsqueeze(1).broadcast_to([P, TOPK, TOPK]), ALU.mult)
                    dve.drain()
                    V.tensor_reduce(picked[:, :, :].rearrange("p t k -> p (t k)"), hit[:, :, :], X, ALU.add)
                dve.drain()
                V.tensor_scalar(pick_a[:, :, :], pick_a[:, :, :], float(KEYS), float(layer * EXPERTS),
                                ALU.mult, ALU.add)
                dve.drain()
                V.tensor_tensor(expert[:, :, ds(h * TOPK, TOPK)], pick_a[:, :, :], pick_b[:, :, :], ALU.add)\
                 .then_inc(s_top, 1)

            def gates(layer, h):
                dve.wait_ge(s_be, layer * PH + h + 1)
                V.tensor_reduce(gate_s[:, :], best_e[:, :, :], X, ALU.add)
                dve.drain()
                V.reciprocal(gate_r[:, :], gate_s[:, :])
                dve.drain()
                V.tensor_tensor(gate[:, :, ds(h * TOPK, TOPK)], best_e[:, :, :],
                                gate_r[:, :].unsqueeze(2).broadcast_to([P, TILES, TOPK]), ALU.mult)

            def dot(layer, g, k):
                b = k % RING
                base = layer * GROUPS
                dve.wait_ge(s_ug[b], 16 * ((base + g) * 2 + k // RING + 1))
                rows = u_rows[:, b, :].rearrange("p (c n) -> p c n", c=2)
                V.tensor_tensor_reduce(out=rows, in0=px, in1=rows, scale=1.0,
                                       scalar=0.0, op0=ALU.mult, op1=ALU.add, accum_out=hid[:, k:k + 1])\
                 .then_inc(s_dot, 1)

            gate_flat = gate[:, :, :].rearrange("p t n -> p (t n)")

            def weights(layer, g):
                dve.wait_ge(s_gelu, layer * GROUPS + g + 1)
                V.tensor_tensor(wts[:, :], act_hid[:, :], gate_flat[:, ds(g * TOPK, TOPK)], ALU.mult)\
                 .then_inc(s_wts, 1)

            def dots(layer, g, choose=None):
                for k in range(TOPK):
                    dot(layer, g, k)
                    if choose is not None:
                        if k == 5:
                            key_top16(layer, choose)
                        if k == 8:
                            dve.drain()
                            pair_top16()
                        if k == 10:
                            expert_numbers(layer, choose)
                        if k == 12:
                            gates(layer, choose)
                weights(layer, g)

            def load_px(t):
                dve.drain()
                V.tensor_copy(px, nat[:, t, :].rearrange("p (c n) -> p c n", c=2))
                dve.drain()

            def peer(layer):
                n = norm_no(layer, 0, 0)
                dve.wait_ge(s_y, (layer + 1) * PAIRS)
                for t in range(TILES):
                    norm(n + t, y01[:, t, :, :], t)
                load_px(0)
                key_top16(layer, 0)
                dve.drain()
                pair_top16()
                expert_numbers(layer, 0)
                gates(layer, 0)
                dots(layer, 0, choose=1)
                with dve.Fori(1, PH - 1) as g:
                    dots(layer, g, choose=g + 1)
                dots(layer, PH - 1)
                load_px(1)
                dots(layer, PH)
                base = layer * GROUPS * TOPK
                dve.wait_ge(s_acc, products_done(base + PH * TOPK))
                norm(n + 2, ffn[0], 0)
                with dve.Fori(PH + 1, GROUPS) as g:
                    dots(layer, g)
                dve.wait_ge(s_acc, products_done(base + GROUPS * TOPK))
                norm(n + 3, ffn[1], 1)

            peer(0)

            def rope(dst, scale):
                V.scalar_tensor_tensor(out=rope_a[:, :], in0=qk_ps[0:2 * ROPE, 0, :], scalar=scale,
                                       in1=cos_t[:, :], op0=ALU.mult, op1=ALU.mult)
                V.scalar_tensor_tensor(out=rope_b[:, :], in0=qk_ps[0:2 * ROPE, 1, :], scalar=scale,
                                       in1=sin_t[:, :], op0=ALU.mult, op1=ALU.mult)
                dve.drain()
                return V.tensor_tensor(dst[:, :], rope_a[:, :], rope_b[:, :], ALU.add)

            def latent_norm(t):
                dve.wait_ge(s_css, t + 1)
                V.tensor_scalar(c_ms[:, :], c_ss[:, :], 1.0 / RANK, EPS, ALU.mult, ALU.add).then_inc(s_cms, 1)
                dve.wait_ge(s_cstd, t + 1)
                V.reciprocal(c_rstd[:, :], c_std[:, :])
                dve.drain()
                if t:
                    dve.wait_ge(s_ctr, t)
                for s in range(2):
                    last = V.tensor_scalar(cn[:, s * RK:(s + 1) * RK, :].rearrange("p c n -> p (c n)"),
                                           b_att[t][:, s * RANK:(s + 1) * RANK], c_rstd[:, s:s + 1], None, ALU.mult)
                last.then_inc(s_cn, 1)

            def store_cT(t):
                dve.wait_ge(s_ctr, t + 1)
                src = b_vo[:, :] if t == 0 else b_att[0]
                V.tensor_tensor(cT[:, :, t * P:(t + 1) * P], src.rearrange("p (c n) -> p c n", c=2 * RK),
                                norm_col[:, :].unsqueeze(2).broadcast_to([P, 2 * RK, P]), ALU.mult).then_inc(s_cT, 1)

            latent_norm(0)
            store_cT(0)
            latent_norm(1)
            store_cT(1)
            dve.wait_ge(s_kpps, 1)
            rope(kpe, 1.0).then_inc(s_kpsb, 1)

            def rope_q(j):
                dve.wait_ge(s_peps, j + 1)
                rope(qpe, MLA_SCALE).then_inc(s_pesb, 1)

            def pair_mla(j, last_pair=False):
                jj = PAIRS + j
                for i in range(2):
                    softmax(jj, i)
                if not last_pair:
                    rope_q(j + 1)
                for i in range(2):
                    normalise(jj, i)
                for i in range(2):
                    store_probsT(jj, i)

            rope_q(0)
            with dve.Fori(0, PAIRS - 1) as j:
                pair_mla(j)
            pair_mla(PAIRS - 1, True)
            peer(1)


_INS = ['x', 'na_w_in', 'na_rel_bias', 'na_w_out', 'mla_w_in', 'mla_q_norm', 'mla_kv_norm', 'mla_w_q_up',
        'mla_w_kv_up', 'mla_w_out', 'peer_w_q', 'peer_sub_keys', 'peer_u', 'peer_v', 'ln_mix_g', 'ln_mix_b',
        'ln_ffn_g', 'ln_ffn_b']
_OUTS = [((1, TOK, D), 'float32')]


def kernel(**inputs):
    import numpy as _np
    import concourse.bacc as _bacc
    from concourse import mybir as _mybir
    from concourse.bass_utils import run_bass_kernel_spmd as _run

    half = ROPE // 2
    freq = (10000.0 ** (-_np.arange(half) * 2.0 / ROPE)).astype(_np.float32)
    angle = freq[:, None] * _np.arange(TOK, dtype=_np.float32)[None, :]
    cos, sin = _np.cos(angle), _np.sin(angle)
    tables = {'rope_cos': _np.concatenate([cos, cos, cos, cos], axis=0),
              'rope_sin': _np.concatenate([-sin, sin, -sin, sin], axis=0)}

    nc = _bacc.Bacc("TRN2", target_bir_lowering=False, num_devices=1)
    arrays, args = {}, []
    for name in _INS + list(tables):
        a = _np.ascontiguousarray(tables[name] if name in tables else inputs[name])
        arrays[f"in_{name}_dram"] = a
        args.append(nc.dram_tensor(f"in_{name}_dram", a.shape, _mybir.dt.from_np(a.dtype), kind="ExternalInput").ap())
    for i, (shape, dtype) in enumerate(_OUTS):
        dt = _mybir.dt.from_np(_np.dtype(dtype))
        args.append(nc.dram_tensor(f"out_{i}_dram", shape, dt, kind="ExternalOutput").ap())
    program(nc, *args)
    r = _run(nc, [arrays], core_ids=[0])
    return r.results[0]["out_0_dram"]
```

```python
import concourse.bass as bass
from concourse import mybir
from contextlib import ExitStack

P = 128
D = 1024
TOK = 256
TILES = TOK // P
DK = D // P
LAYERS = 2
ALPHA = (2.0 * LAYERS) ** 0.25
EPS = 1e-5

GRID_W = 64
ROWS = TOK // GRID_W
NA_KH, NA_KW = 8, 16
HEADS = 16
PAIRS = HEADS // 2
HD = 64
PAIR = 2 * HD
NA_SCALE = HD ** -0.5
BIAS_W = 2 * NA_KW - 1
BIAS_H = 2 * NA_KH - 1

RANK = 256
RK = RANK // P
ROPE = 32
QW = HD + ROPE
KVW = 2 * HD
MLA_SCALE = QW ** -0.5

PH = 8
KEYS = 128
DKEY = 128
EXPERTS = KEYS * KEYS
TOPK = 16
GROUPS = TILES * PH
CHOICES = PH + 2
RING = 8
NEG = -1e30


def program(nc, x, na_w_in, rel_bias, na_w_out, mla_w_in, mla_q_norm, mla_kv_norm, w_q_up, w_kv_up,
            mla_w_out, peer_w_q, sub_keys, peer_u, peer_v, ln_mix_g, ln_mix_b, ln_ffn_g, ln_ffn_b,
            rope_cos, rope_sin, out):
    f32 = mybir.dt.float32
    i32 = mybir.dt.int32
    u32 = mybir.dt.uint32
    ALU = mybir.AluOpType
    ACT = mybir.ActivationFunctionType
    X = mybir.AxisListType.X
    ds = bass.ds

    with ExitStack() as ctx:
        def sb(name, shape, dt=f32):
            return ctx.enter_context(nc.sbuf_tensor(name, shape, dt))

        def bank(name):
            return ctx.enter_context(nc.psum_tensor(name, [P, 512], f32))

        def sem(name):
            return ctx.enter_context(nc.semaphore(name))

        ident = sb("ident", [P, P])
        alpha_ident = sb("alpha_ident", [P, P])
        iota16 = sb("iota16", [P, TOPK])
        na_mask = sb("na_mask", [P, GRID_W])
        eps_col = sb("eps_col", [P, 1])
        keys = sb("keys", [P, LAYERS * 2, DKEY])
        keysT = sb("keysT", [P, LAYERS * 2, KEYS])
        g_col = sb("g_col", [P, 3, DK])
        b_col = sb("b_col", [P, 3, DK])
        norm_col = sb("norm_col", [P, 2 * RK])
        cos_t = sb("cos_t", [2 * ROPE, TOK])
        sin_t = sb("sin_t", [2 * ROPE, TOK])
        nat = sb("nat", [P, TILES, D])
        hT = sb("hT", [P, DK, TOK])
        g_row = sb("g_row", [P, D])
        b_row = sb("b_row", [P, D])
        ln_stats = sb("ln_stats", [P, TILES, 2, 6])
        ln_mv = sb("ln_mv", [P, TILES, 2])
        ln_std = sb("ln_std", [P, TILES])
        ln_rstd = sb("ln_rstd", [P, TILES])
        w_qk = sb("w_qk", [P, 2, DK, PAIR])
        w_v = sb("w_v", [P, DK, PAIR])
        w_o = sb("w_o", [P, D])
        shared = sb("shared", [P, 2, TILES, 2, ROWS, GRID_W])
        bias_raw = shared[:, 0, :, :, :, :]
        bias = shared[:, 1, :, :, :, :]
        w_lat = sb("w_lat", [P, DK, 2 * RANK + ROPE])
        w_kpe = sb("w_kpe", [P, DK, 2, 2, ROPE])
        w_qn = sb("w_qn", [P, RK, 2, HD])
        w_qr = sb("w_qr", [P, RK, 2, ROPE])
        w_qsw = sb("w_qsw", [P, RK, 2, ROPE])
        w_kn = sb("w_kn", [P, RK, 2, HD])
        w_vu = sb("w_vu", [P, RK, 2, HD])
        cn = sb("cn", [P, 2 * RK, P])
        cT = sb("cT", [P, 2 * RK, TOK])
        sq_junk = sb("sq_junk", [P, 2, RANK])
        c_ss = sb("c_ss", [P, 2])
        c_ms = sb("c_ms", [P, 2])
        c_std = sb("c_std", [P, 2])
        c_rstd = sb("c_rstd", [P, 2])
        kpe = sb("kpe", [2 * ROPE, TOK])
        qpe = sb("qpe", [2 * ROPE, TOK])
        rope_a = sb("rope_a", [2 * ROPE, TOK])
        rope_b = sb("rope_b", [2 * ROPE, TOK])
        qk = sb("qk", [P, 2, TOK])
        v_sb = sb("v_sb", [P, TILES, PAIR])
        logits = [sb(f"logits{i}", [P, TILES, TOK]) for i in range(2)]
        probs = [sb(f"probs{i}", [P, TILES, TOK]) for i in range(2)]
        probsT = [sb(f"probsT{i}", [P, TILES, TOK]) for i in range(2)]
        nmax = sb("nmax", [P, 2, TILES])
        psum_row = sb("psum_row", [P, 2, TILES])
        rsum = sb("rsum", [P, 2, TILES])
        oT = sb("oT", [P, TOK])
        w_pq = sb("w_pq", [P, DK, 2 * DKEY])
        qT = sb("qT", [P, 2, TOK])
        key_top = sb("key_top", [P, TILES, 2, TOPK])
        key_idx = sb("key_idx", [P, TILES, 2, TOPK], u32)
        key_idxf = sb("key_idxf", [P, TILES, 2, TOPK])
        key_left = sb("key_left", [P, TILES, 2, KEYS])
        cand = sb("cand", [P, TILES, TOPK, TOPK])
        cand_left = sb("cand_left", [P, TILES, TOPK * TOPK])
        best = sb("best", [P, TILES, TOPK])
        pos = sb("pos", [P, TILES, TOPK], u32)
        pos_ab = sb("pos_ab", [P, TILES, 2, TOPK], u32)
        pos_abf = sb("pos_abf", [P, TILES, 2, TOPK])
        hit = sb("hit", [P, TILES, 2, TOPK, TOPK])
        pick = sb("pick", [P, TILES, 2, TOPK])
        best_d = sb("best_d", [P, TILES, TOPK])
        best_e = sb("best_e", [P, TILES, TOPK])
        gate_s = sb("gate_s", [P, TILES])
        gate_r = sb("gate_r", [P, TILES])
        gate = sb("gate", [P, TILES, PH * TOPK])
        expert = sb("expert", [P, TILES, PH * TOPK], i32)
        idx_u = sb("idx_u", [P, 2, RING], i32)
        idx_v = sb("idx_v", [P, 2, RING], i32)
        u_rows = sb("u_rows", [P, RING, D])
        v_rows = sb("v_rows", [P, RING, D])
        hid = sb("hid", [P, TOPK])
        act_hid = sb("act_hid", [P, TOPK])
        wts = sb("wts", [P, TOPK])
        diag = shared[:, :, :, :, :, :].rearrange("p a t i r c -> p (a t i r c)").rearrange("p (k n) -> p k n", k=TOPK)
        y01 = ctx.enter_context(nc.psum_tensor("y01", [P, TILES, 2, 512], f32))
        b_qk = bank("b_qk")
        b_vo = bank("b_vo")
        att = ctx.enter_context(nc.psum_tensor("att", [P, 2, 512], f32))
        b_att = [att[:, i, :] for i in range(2)]
        px = y01[:, 0, :, :]
        ffn = [y01[:, 1, :, :], att[:, :, :]]
        v_ps = b_vo[:, 0:TILES * PAIR].rearrange("p (t n) -> p t n", t=TILES)
        oT_ps = att[:, 0, 0:TOK]
        qk_ps = b_qk[:, :].rearrange("p (s n) -> p s n", s=2)
        scores_ps = b_vo[:, :].rearrange("p (t c n) -> p t c n", t=TILES, c=2)
        mix_banks = [(att[:, 0, :], att[:, 1, :]), (y01[:, 0, 0, :], y01[:, 0, 1, :])]
        ffn_banks = (b_qk[:, :], b_vo[:, :])
        first_q_ps = [qk_ps[:, :, 0:P], att[:, 0, 0:2 * P].rearrange("p (c n) -> p c n", c=2)]
        lat_ps = [b_qk[:, :], att[:, 0, :]]
        kpe_ps = [b[0:2 * ROPE, 0:2 * P].rearrange("p (s n) -> p s n", s=2) for b in (b_vo[:, :], att[:, 1, :])]
        cT_ps = b_vo[:, :]

        s_x = sem("x_loaded"); s_keys = sem("sub_keys_loaded"); s_small = sem("small_loaded"); s_lat = sem("w_lat_loaded")
        s_wqk = sem("w_qk_loaded"); s_wv = sem("w_v_loaded"); s_wo = sem("w_o_loaded")
        s_wqu = sem("w_qu_loaded"); s_wqr = sem("w_q_rope_loaded"); s_wkvu = sem("w_kvu_loaded"); s_braw = sem("bias_raw_loaded")
        s_rows = sem("ln_rows_loaded"); s_wpq = sem("w_pq_loaded"); s_out = sem("out_stored")
        s_const = sem("constants_made"); s_bias = sem("bias_masked"); s_swap = sem("rope_cols_swapped")
        s_xtr = sem("x_transposed_ps"); s_xT = sem("x_transposed_sb"); s_ktr = sem("keysT_ps"); s_kT = sem("keysT_sb")
        s_qkps = sem("qk_in_psum"); s_qksb = sem("qk_in_sbuf")
        s_vps = sem("v_in_psum"); s_vsb = sem("v_in_sbuf")
        s_sc = sem("logits_in_psum"); s_max = sem("row_max_ready"); s_exp = sem("exp_done")
        s_prob = sem("probs_ready"); s_ptps = sem("probsT_in_psum"); s_ptsb = sem("probsT_in_sbuf")
        s_pv = sem("pv_in_psum"); s_oT = sem("oT_in_sbuf"); s_y = sem("out_product_done")
        s_badd = sem("bias_added")
        s_peps = sem("q_rope_in_psum"); s_pesb = sem("q_rope_done")
        s_cps = sem("latents_in_psum"); s_css = sem("latent_squares"); s_cms = sem("latent_ms")
        s_cstd = sem("latent_std"); s_cn = sem("latents_normed"); s_ctr = sem("latentsT_in_psum")
        s_cT = sem("latentsT_in_sbuf"); s_kpps = sem("k_rope_in_psum"); s_kpsb = sem("k_rope_done")
        s_var = sem("ln_var_ready"); s_std = sem("ln_std_ready"); s_xhat = sem("ln_xhat_ready")
        s_tr = sem("ln_transposed_ps"); s_hT = sem("ln_hT_ready"); s_nat = sem("ln_nat_ready")
        s_px = sem("px_ready")
        s_qTps = sem("peer_q_in_psum"); s_qTsb = sem("peer_q_in_sbuf"); s_ks = sem("key_scores_ready")
        s_bd = sem("best_minus_max"); s_be = sem("best_exp")
        s_top = [sem(f"experts_chosen_tile{t}") for t in range(TILES)]
        s_q0ps = sem("first_q_tile0_in_psum"); s_q0sb = sem("first_q_tile0_in_sbuf")
        s_ix = sem("indices_copied")
        s_ug = [sem(f"u_rows_landed{i}") for i in range(RING)]
        s_vg = [sem(f"v_rows_landed{i}") for i in range(RING)]
        s_dot = sem("dot_done"); s_gelu = sem("gelu_done"); s_wts = sem("weights_ready")
        s_diag = sem("diag_ready"); s_acc = sem("v_accumulated"); s_pool = sem("pool_step"); s_dstep = sem("dve_step")

        block = ctx.enter_context(nc.Block())

        def norm_no(layer, ffn_norm, tile):
            return 4 * layer + 2 * ffn_norm + tile

        def rows_reversed(ap):
            return bass.AP(ap.tensor, ap.offset + GRID_W - 1, [list(ap.ap[0]), [GRID_W, ROWS], [-1, GRID_W]])

        def choice_no(step, tiles):
            if isinstance(step, int) and (step == 0 or (step, tiles) == (1, (1,))):
                return step
            return step + 1

        def dots_done(n):
            return n + RING

        def products_done(n):
            return n + RING

        @block.sync
        def _(sp):
            for t in range(TILES):
                sp.dma_start(nat[:, t, :], x[0, t * P:(t + 1) * P, :]).then_inc(s_x, 16)

            w_in3 = na_w_in[0].rearrange("(k p) (s c) -> s p k c", p=P, s=3)

            def load_na_qk(j):
                for s in range(2):
                    sp.dma_start(w_qk[:, s, :, :], w_in3[s][:, :, ds(j * PAIR, PAIR)]).then_inc(s_wqk, 16)

            def load_na_v(j):
                sp.dma_start(w_v[:, :, :], w_in3[2][:, :, ds(j * PAIR, PAIR)]).then_inc(s_wv, 16)

            def load_out_rows(j, w):
                sp.dma_start(w_o[:, :], w[ds(j * PAIR, PAIR), :]).then_inc(s_wo, 16)

            def load_bias(j):
                for t in range(TILES):
                    for rho in range(2):
                        for i in range(2):
                            r = 2 * t + rho
                            first = (i * BIAS_H + NA_KH - 1 - r) * BIAS_W + NA_KW - GRID_W
                            src = bass.AP(rel_bias.tensor, j * (2 * BIAS_H * BIAS_W) + first,
                                          [[1, GRID_W], [BIAS_W, ROWS], [1, GRID_W]])
                            sp.dma_start(bias_raw[rho * GRID_W:(rho + 1) * GRID_W, t, i, :, :], src)\
                              .then_inc(s_braw, 16)

            load_na_qk(0)
            load_na_v(0)
            load_bias(0)
            sp.dma_start(keys[:, :, :], sub_keys.rearrange("l c n d -> n (l c) d")).then_inc(s_keys, 16)
            for n, (g, b) in enumerate(((ln_mix_g[0], ln_mix_b[0]), (ln_ffn_g[0], ln_ffn_b[0]),
                                        (ln_mix_g[1], ln_mix_b[1]))):
                sp.dma_start(g_col[:, n, :], g.rearrange("(k p) -> p k", p=P),
                             allow_slow_non_contiguous=True).then_inc(s_small, 16)
                sp.dma_start(b_col[:, n, :], b.rearrange("(k p) -> p k", p=P),
                             allow_slow_non_contiguous=True).then_inc(s_small, 16)
            sp.dma_start(norm_col[:, 0:RK], mla_q_norm[0].rearrange("(k p) -> p k", p=P),
                         allow_slow_non_contiguous=True).then_inc(s_small, 16)
            sp.dma_start(norm_col[:, RK:], mla_kv_norm[0].rearrange("(k p) -> p k", p=P),
                         allow_slow_non_contiguous=True).then_inc(s_small, 16)
            sp.dma_start(cos_t[:, :], rope_cos).then_inc(s_small, 16)
            sp.dma_start(sin_t[:, :], rope_sin).then_inc(s_small, 16)

            def load_norm_rows(n, g, b):
                if n:
                    sp.wait_ge(s_nat, 2 * n)
                sp.dma_start(g_row[:, :], g.partition_broadcast(P)).then_inc(s_rows, 16)
                sp.dma_start(b_row[:, :], b.partition_broadcast(P)).then_inc(s_rows, 16)

            load_norm_rows(0, ln_mix_g[0:1, :], ln_mix_b[0:1, :])

            with sp.Fori(1, PAIRS) as j:
                sp.wait_ge(s_qkps, j)
                load_na_qk(j)
                sp.wait_ge(s_vps, j)
                load_na_v(j)
                sp.wait_ge(s_bias, j)
                load_bias(j)
                sp.wait_ge(s_ptps, 2 * j - 1)
                load_out_rows(j - 1, na_w_out[0])
            sp.wait_ge(s_ptps, 2 * PAIRS - 1)
            load_out_rows(PAIRS - 1, na_w_out[0])

            def load_pq(layer, h):
                sp.dma_start(w_pq[:, :, :], peer_w_q[layer].rearrange("(k p) n -> p k n", p=P)
                             [:, :, ds(h * 2 * DKEY, 2 * DKEY)]).then_inc(s_wpq, 16)

            def peer_loads(layer):
                with sp.Fori(1, PH) as h:
                    sp.wait_ge(s_qTps, layer * PH + h)
                    load_pq(layer, h)

            load_pq(0, 0)
            sp.dma_start(w_lat[:, :, :], mla_w_in[0].rearrange("(k p) n -> p k n", p=P)).then_inc(s_lat, 16)
            def load_mla_q(j):
                cols = w_q_up[0].rearrange("(k p) n -> p k n", p=P)
                for i in range(2):
                    sp.dma_start(w_qr[:, :, i, :], cols[:, :, ds(j * 2 * QW + i * QW + HD, ROPE)]).then_inc(s_wqr, 16)
                for i in range(2):
                    sp.dma_start(w_qn[:, :, i, :], cols[:, :, ds(j * 2 * QW + i * QW, HD)]).then_inc(s_wqu, 16)

            def load_mla_kv(j):
                cols = w_kv_up[0].rearrange("(k p) n -> p k n", p=P)
                for i in range(2):
                    for part, w in enumerate((w_kn, w_vu)):
                        sp.dma_start(w[:, :, i, :], cols[:, :, ds(j * 2 * KVW + i * KVW + part * HD, HD)])\
                          .then_inc(s_wkvu, 16)

            load_mla_q(0)
            load_mla_kv(0)
            load_norm_rows(1, ln_ffn_g[0:1, :], ln_ffn_b[0:1, :])
            peer_loads(0)
            sp.wait_ge(s_qTps, PH)
            load_pq(1, 0)
            load_norm_rows(2, ln_mix_g[1:2, :], ln_mix_b[1:2, :])
            with sp.Fori(1, PAIRS) as j:
                sp.wait_ge(s_qkps, PAIRS + j)
                load_mla_q(j)
                sp.wait_ge(s_vps, PAIRS + j)
                load_mla_kv(j)
                sp.wait_ge(s_pv, 2 * (PAIRS + j) - 1)
                load_out_rows(j - 1, mla_w_out[0])
            sp.wait_ge(s_pv, 2 * 2 * PAIRS - 1)
            load_out_rows(PAIRS - 1, mla_w_out[0])
            load_norm_rows(3, ln_ffn_g[1:2, :], ln_ffn_b[1:2, :])
            peer_loads(1)
            for t in range(TILES):
                sp.wait_ge(s_nat, norm_no(1, 1, t) + 1)
                sp.dma_start(out[0, t * P:(t + 1) * P, :], nat[:, t, :]).then_inc(s_out, 16)
            sp.wait_ge(s_out, 16 * TILES)

        @block.gpsimd
        def _(pool):
            pool.memset(ident[:, :], 0.0).then_inc(s_pool, 1)
            pool.memset(alpha_ident[:, :], 0.0).then_inc(s_pool, 1)
            pool.memset(na_mask[:, :], 0.0).then_inc(s_pool, 1)
            pool.memset(eps_col[:, :], EPS).then_inc(s_const, 1)
            pool.iota(iota16[:, :], [[1, TOPK]], base=0, channel_multiplier=0,
                      allow_small_or_imprecise_dtypes=True).then_inc(s_const, 1)
            pool.wait_ge(s_pool, 3)
            pool.affine_select(out=ident[:, :], in_=ident[:, :], compare_op=ALU.not_equal, fill=1.0,
                               base=0, pattern=[[-1, P]], channel_multiplier=1).then_inc(s_const, 1)
            pool.affine_select(out=alpha_ident[:, :], in_=alpha_ident[:, :], compare_op=ALU.not_equal,
                               fill=ALPHA, base=0, pattern=[[-1, P]], channel_multiplier=1).then_inc(s_const, 1)
            pool.wait_ge(s_const, 4)
            half, edge = NA_KW // 2, GRID_W - NA_KW
            for rho in range(2):
                left = na_mask[rho * GRID_W:(rho + 1) * GRID_W, 0:edge]
                pool.affine_select(out=left, in_=left, compare_op=ALU.is_ge, fill=NEG,
                                   base=half - (GRID_W - 1), pattern=[[1, edge]], channel_multiplier=1)\
                    .then_inc(s_pool, 1)
                pool.wait_ge(s_pool, 4 + 2 * rho)
                right = na_mask[rho * GRID_W:(rho + 1) * GRID_W, NA_KW:GRID_W]
                pool.affine_select(out=right, in_=right, compare_op=ALU.is_ge, fill=NEG,
                                   base=half - 1 - NA_KW + GRID_W - 1, pattern=[[-1, edge]],
                                   channel_multiplier=-1).then_inc(s_pool, 1)
                pool.wait_ge(s_pool, 5 + 2 * rho)

            rows = TILES * 2 * ROWS
            mask_b = na_mask[:, :].unsqueeze(1).broadcast_to([P, rows, GRID_W])

            def mask_bias(j, first=False):
                pool.wait_ge(s_braw, 128 * (j + 1))
                if not first:
                    pool.wait_ge(s_badd, 2 * j)
                nc.gpsimd.tensor_tensor(bias.rearrange("p t i r c -> p (t i r) c"),
                                        bias_raw.rearrange("p t i r c -> p (t i r) c"),
                                        mask_b, ALU.add).then_inc(s_bias, 1)

            mask_bias(0, True)
            with pool.Fori(1, PAIRS) as j:
                mask_bias(j)

            expert_flat = expert[:, :, :].rearrange("p t n -> p (t n)")

            def copy_indices(dst, half_no, group):
                nc.gpsimd.tensor_copy(dst[:, half_no, :],
                                      expert_flat[:, ds(group * TOPK + half_no * RING, RING)]).then_inc(s_ix, 1)

            u_table = peer_u.rearrange("l e d -> (l e) d")
            v_table = peer_v.rearrange("l e d -> (l e) d")

            def gather_group(layer, g, copies, heads=None, with_u=True, with_v=True):
                base = layer * GROUPS * TOPK
                if heads is not None:
                    pool.wait_ge(s_top[0], layer * PH + heads)
                    pool.sem_inc(s_pool, 1)
                for half_no in range(2):
                    if with_u:
                        copy_indices(idx_u, half_no, g)
                        copies = copies + 1
                    if with_v:
                        copy_indices(idx_v, half_no, g - 1)
                        copies = copies + 1
                    pool.wait_ge(s_ix, copies)
                    pool.sem_inc(s_pool, 1)
                    for b in range(RING):
                        k = half_no * RING + b
                        if with_u:
                            pool.wait_ge(s_dot, dots_done(base + g * TOPK + k + 1 - RING))
                            pool.sem_inc(s_pool, 1)
                            pool.indirect_dma_start(u_rows[:, b, :], None, u_table,
                                                    bass.IndirectOffsetOnAxis(ap=idx_u[:, half_no, b:b + 1], axis=0))\
                                .then_inc(s_ug[b], 16)
                        if with_v:
                            pool.wait_ge(s_acc, products_done(base + (g - 1) * TOPK + k + 1 - RING))
                            pool.sem_inc(s_pool, 1)
                            pool.indirect_dma_start(v_rows[:, b, :], None, v_table,
                                                    bass.IndirectOffsetOnAxis(ap=idx_v[:, half_no, b:b + 1], axis=0))\
                                .then_inc(s_vg[b], 16)

            def gathers(layer):
                start = layer * GROUPS * 4
                gather_group(layer, 0, start, heads=1, with_v=False)
                with pool.Fori(1, PH) as g:
                    gather_group(layer, g, start + 4 * g - 2, heads=g + 1)
                pool.wait_ge(s_top[1], (layer + 1) * PH)
                pool.sem_inc(s_pool, 1)
                with pool.Fori(PH, GROUPS) as g:
                    gather_group(layer, g, start + 4 * g - 2)
                gather_group(layer, GROUPS, start + 4 * GROUPS - 2, with_u=False)

            hr = ROPE // 2
            pool.wait_ge(s_lat, 16)
            pool.sem_inc(s_pool, 1)
            for rep in range(2):
                nc.gpsimd.tensor_copy(w_kpe[:, :, 0, rep, :], w_lat[:, :, 2 * RANK:])
                for part in range(2):
                    src = 2 * RANK + (1 - part) * hr
                    last = nc.gpsimd.tensor_copy(w_kpe[:, :, 1, rep, part * hr:(part + 1) * hr],
                                                 w_lat[:, :, src:src + hr])
            last.then_inc(s_swap, 1)

            def swap_q_rope(j, first=False):
                pool.wait_ge(s_wqr, 32 * (j + 1))
                pool.sem_inc(s_pool, 1)
                if not first:
                    pool.wait_ge(s_peps, j)
                    pool.sem_inc(s_pool, 1)
                for part in range(2):
                    src = (1 - part) * hr
                    last = nc.gpsimd.tensor_copy(w_qsw[:, :, :, part * hr:(part + 1) * hr],
                                                 w_qr[:, :, :, src:src + hr])
                last.then_inc(s_swap, 1)

            swap_q_rope(0, True)
            gathers(0)
            with pool.Fori(1, PAIRS) as j:
                swap_q_rope(j)
            gathers(1)

        @block.tensor
        def _(pe):
            pe.sem_inc(s_acc, RING)
            pe.wait_ge(s_const, 4)
            pe.wait_ge(s_x, 16 * TILES)
            for t in range(TILES):
                for half in range(2):
                    n = 2 * t + half
                    if n >= 2:
                        pe.wait_ge(s_xT, n - 1)
                    for c in range(4):
                        k = 4 * half + c
                        last = nc.tensor.transpose(b_att[n % 2][:, c * P:(c + 1) * P],
                                                   nat[:, t, k * P:(k + 1) * P], ident[:, :])
                    last.then_inc(s_xtr, 1)
            def seed(acc, t):
                for c in range(2):
                    nc.tensor.matmul(acc[:, c, :], alpha_ident[:, :], nat[:, t, c * 512:(c + 1) * 512],
                                            start=True, stop=False)

            def scores_na(j, i):
                for t in range(TILES):
                    last = nc.tensor.matmul(b_att[i][:, t * TOK:(t + 1) * TOK],
                                            qk[i * HD:(i + 1) * HD, 0, t * P:(t + 1) * P],
                                            qk[i * HD:(i + 1) * HD, 1, :], start=True, stop=True)
                last.then_inc(s_sc, 1)

            def scores_mla(j, i):
                for t in range(TILES):
                    nc.tensor.matmul(b_att[i][:, t * TOK:(t + 1) * TOK],
                                     qk[i * HD:(i + 1) * HD, 0, t * P:(t + 1) * P],
                                     qk[i * HD:(i + 1) * HD, 1, :], start=True, stop=False)
                    last = nc.tensor.matmul(b_att[i][:, t * TOK:(t + 1) * TOK],
                                            qpe[i * ROPE:(i + 1) * ROPE, t * P:(t + 1) * P],
                                            kpe[i * ROPE:(i + 1) * ROPE, :], start=False, stop=True)
                last.then_inc(s_sc, 1)

            def transpose_probs(jj, i):
                pe.wait_ge(s_prob, 2 * jj + i + 1)
                for t in range(TILES):
                    for kt in range(TILES):
                        last = nc.tensor.transpose(b_att[i][:, kt * TOK + t * P:kt * TOK + (t + 1) * P],
                                                   probs[i][:, t, kt * P:(kt + 1) * P], ident[:, :])
                last.then_inc(s_ptps, 1)

            def pv(jj, i):
                if i == 0:
                    pe.wait_ge(s_ptsb, 2 * jj + 2)
                for kt in range(TILES):
                    last = nc.tensor.matmul(oT_ps[i * HD:(i + 1) * HD, :], v_sb[:, kt, i * HD:(i + 1) * HD],
                                            probsT[i][:, kt, :], start=(kt == 0), stop=(kt == TILES - 1))
                last.then_inc(s_pv, 1)

            def out_product(jj, tiles=(0, 1), last_pair=False):
                if tiles[0] == 0:
                    pe.wait_ge(s_wo, 16 * (jj + 1))
                    pe.wait_ge(s_oT, jj + 1)
                for t in tiles:
                    for c in range(2):
                        last = nc.tensor.matmul(y01[:, t, c, :], oT[:, t * P:(t + 1) * P],
                                                w_o[:, c * 512:(c + 1) * 512], start=False, stop=last_pair)
                if tiles[-1] == 1:
                    last.then_inc(s_y, 1)

            def project_na(j, s):
                if s == 0:
                    pe.wait_ge(s_wqk, 32 * (j + 1))
                for k in range(DK):
                    last = nc.tensor.matmul(qk_ps[:, s, :], w_qk[:, s, k, :], hT[:, k, :],
                                            start=(k == 0), stop=(k == DK - 1))
                if s == 1:
                    last.then_inc(s_qkps, 1)

            def project_v_na(j):
                pe.wait_ge(s_wv, 16 * (j + 1))
                for t in range(TILES):
                    for k in range(DK):
                        last = nc.tensor.matmul(v_ps[:, t, :], hT[:, k, t * P:(t + 1) * P], w_v[:, k, :],
                                                start=(k == 0), stop=(k == DK - 1))
                last.then_inc(s_vps, 1)

            def pair_na(j, first=False, last_pair=False):
                pe.wait_ge(s_qksb, j + 1)
                if not first:
                    pe.wait_ge(s_oT, j)
                for i in range(2):
                    scores_na(j, i)
                if not first:
                    out_product(j - 1)
                if not last_pair:
                    project_na(j + 1, 0)
                for i in range(2):
                    transpose_probs(j, i)
                if not last_pair:
                    project_na(j + 1, 1)
                pe.wait_ge(s_vsb, j + 1)
                for i in range(2):
                    pv(j, i)
                if not last_pair:
                    project_v_na(j + 1)

            for t in range(TILES):
                seed(y01[:, t, :, :], t)
            pe.wait_ge(s_xT, 4)
            for s in range(2):
                project_na(0, s)
            project_v_na(0)
            pair_na(0, first=True)
            with pe.Fori(1, PAIRS - 1) as j:
                pair_na(j)
            pair_na(PAIRS - 1, last_pair=True)
            out_product(PAIRS - 1, last_pair=True)
            pe.wait_ge(s_keys, 16)
            for n in range(LAYERS * 2):
                last = nc.tensor.transpose(b_qk[:, n * P:(n + 1) * P], keys[:, n, :], ident[:, :])
            last.then_inc(s_ktr, 1)

            def norm_transposes(n, t, banks):
                pe.wait_ge(s_xhat, n + 1)
                for half in range(2):
                    for c in range(4):
                        k = 4 * half + c
                        last = nc.tensor.transpose(banks[half][:, c * P:(c + 1) * P],
                                                   nat[:, t, k * P:(k + 1) * P], ident[:, :])
                    last.then_inc(s_tr, 1)

            def peer_queries(layer, h):
                pe.wait_ge(s_wpq, 16 * (layer * PH + h + 1))
                for c in range(2):
                    for k in range(DK):
                        last = nc.tensor.matmul(qk_ps[:, c, :], w_pq[:, k, c * DKEY:(c + 1) * DKEY],
                                                hT[:, k, :], start=(k == 0), stop=(k == DK - 1))
                last.then_inc(s_qTps, 1)

            def first_queries(layer, t):
                for c in range(2):
                    for k in range(DK):
                        last = nc.tensor.matmul(first_q_ps[t][:, c, :], w_pq[:, k, c * DKEY:(c + 1) * DKEY],
                                                hT[:, k, t * P:(t + 1) * P], start=(k == 0), stop=(k == DK - 1))
                last.then_inc(s_q0ps if t == 0 else s_qTps, 1)

            def key_scores(layer, t):
                for c in range(2):
                    last = nc.tensor.matmul(scores_ps[:, t, c, :], qT[:, c, t * P:(t + 1) * P],
                                            keysT[:, 2 * layer + c, :], start=True, stop=True)
                return last

            def score_step(layer, step):
                pe.wait_ge(s_top[0], layer * PH + step)
                pe.wait_ge(s_top[1], layer * PH + step - 1)
                pe.wait_ge(s_qTsb, layer * PH + step)
                last = key_scores(layer, 1)
                if isinstance(step, int) and step == PH:
                    last.then_inc(s_ks, 1)
                    return
                peer_queries(layer, step)
                pe.wait_ge(s_qTsb, layer * PH + step + 1)
                key_scores(layer, 0).then_inc(s_ks, 1)

            def add_experts(layer, tile, g, stop=False):
                base = layer * GROUPS
                for k in range(TOPK):
                    b = k % RING
                    pe.wait_ge(s_diag, (base + g) * TOPK + k + 1)
                    pe.wait_ge(s_vg[b], 16 * ((base + g) * 2 + k // RING + 1))
                    for c in range(2):
                        last = nc.tensor.matmul(ffn[tile][:, c, :], diag[:, k, :],
                                                v_rows[:, b, c * 512:(c + 1) * 512],
                                                start=False, stop=stop and k == TOPK - 1)
                    last.then_inc(s_acc, 1)

            def peer(layer):
                mix = norm_no(layer, 0, 0)
                for t in range(TILES):
                    norm_transposes(mix + t, t, mix_banks[t])
                if layer == 0:
                    pe.wait_ge(s_kT, 1)
                pe.wait_ge(s_wpq, 16 * (layer * PH + 1))
                pe.wait_ge(s_hT, 2 * mix + 2)
                first_queries(layer, 0)
                pe.wait_ge(s_q0sb, layer + 1)
                key_scores(layer, 0).then_inc(s_ks, 1)
                pe.wait_ge(s_hT, 2 * mix + 4)
                first_queries(layer, 1)
                pe.wait_ge(s_nat, mix + 2)
                seed(ffn[0], 0)
                pe.wait_ge(s_qTsb, layer * PH + 1)
                seed(ffn[1], 1)
                pe.wait_ge(s_bd, layer * CHOICES + 1)
                key_scores(layer, 1).then_inc(s_ks, 1)
                peer_queries(layer, 1)
                pe.wait_ge(s_qTsb, layer * PH + 2)
                pe.wait_ge(s_bd, layer * CHOICES + 2)
                key_scores(layer, 0).then_inc(s_ks, 1)
                with pe.Fori(1, PH - 1) as g:
                    score_step(layer, g + 1)
                    add_experts(layer, 0, g - 1)
                score_step(layer, PH)
                add_experts(layer, 0, PH - 2)
                add_experts(layer, 0, PH - 1, stop=True)
                if layer == 0:
                    norm_transposes(norm_no(layer, 1, 0), 0, ffn_banks)
                    pe.wait_ge(s_hT, 2 * norm_no(layer, 1, 0) + 2)
                    latents(0)
                    pe.wait_ge(s_kpsb, 1)
                    latents_transposed(0)
                with pe.Fori(PH + 1, GROUPS) as g:
                    add_experts(layer, 1, g - 1)
                add_experts(layer, 1, GROUPS - 1, stop=True)

            def latents(t):
                if t == 0:
                    pe.wait_ge(s_swap, 1)
                for k in range(DK):
                    last = nc.tensor.matmul(lat_ps[t], hT[:, k, t * P:(t + 1) * P], w_lat[:, k, 0:2 * RANK],
                                            start=(k == 0), stop=(k == DK - 1))
                last.then_inc(s_cps, 1)
                for s in range(2):
                    for k in range(DK):
                        last = nc.tensor.matmul(kpe_ps[t][:, s, :],
                                                w_kpe[:, k, s, :, :].rearrange("p r c -> p (r c)"),
                                                hT[:, k, t * P:(t + 1) * P], start=(k == 0), stop=(k == DK - 1))
                last.then_inc(s_kpps, 1)

            def latents_transposed(t):
                pe.wait_ge(s_cn, t + 1)
                for c in range(2 * RK):
                    last = nc.tensor.transpose(cT_ps[:, c * P:(c + 1) * P], cn[:, c, :], ident[:, :])
                last.then_inc(s_ctr, 1)

            peer(0)
            seed(y01[:, 0, :, :], 0)
            pe.wait_ge(s_cT, 1)
            norm_transposes(norm_no(0, 1, 1), 1, ffn_banks)
            pe.wait_ge(s_hT, 2 * norm_no(0, 1, 1) + 2)
            latents(1)
            latents_transposed(1)
            pe.wait_ge(s_nat, norm_no(0, 1, 1) + 1)
            seed(y01[:, 1, :, :], 1)

            def project_qpe(j):
                pe.wait_ge(s_wqr, 32 * (j + 1))
                pe.wait_ge(s_swap, j + 2)
                for s in range(2):
                    for k in range(RK):
                        w = w_qr if s == 0 else w_qsw
                        last = nc.tensor.matmul(qk_ps[0:2 * ROPE, s, :],
                                                w[:, k, :, :].rearrange("p h n -> p (h n)"), cT[:, k, :],
                                                start=(k == 0), stop=(k == RK - 1))
                last.then_inc(s_peps, 1)

            def project_qk_mla(j):
                pe.wait_ge(s_wqu, 32 * (j + 1))
                pe.wait_ge(s_wkvu, 64 * (j + 1))
                pe.wait_ge(s_pesb, j + 1)
                for s, w in ((0, w_qn), (1, w_kn)):
                    for k in range(RK):
                        last = nc.tensor.matmul(qk_ps[:, s, :], w[:, k, :, :].rearrange("p h n -> p (h n)"), cT[:, RK * s + k, :],
                                                start=(k == 0), stop=(k == RK - 1))
                last.then_inc(s_qkps, 1)

            def project_v_mla(j):
                for t in range(TILES):
                    for k in range(RK):
                        last = nc.tensor.matmul(v_ps[:, t, :], cT[:, RK + k, t * P:(t + 1) * P],
                                                w_vu[:, k, :, :].rearrange("p h n -> p (h n)"), start=(k == 0), stop=(k == RK - 1))
                last.then_inc(s_vps, 1)

            def pair_mla(j, first=False, last_pair=False):
                jj = PAIRS + j
                pe.wait_ge(s_qksb, jj + 1)
                if not first:
                    pe.wait_ge(s_oT, jj)
                for i in range(2):
                    scores_mla(j, i)
                if not first:
                    out_product(jj - 1, (0,))
                if not last_pair:
                    project_qpe(j + 1)
                for i in range(2):
                    transpose_probs(jj, i)
                if not first:
                    out_product(jj - 1, (1,))
                pe.wait_ge(s_vsb, jj + 1)
                for i in range(2):
                    pv(jj, i)
                if not last_pair:
                    project_qk_mla(j + 1)
                    project_v_mla(j + 1)

            pe.wait_ge(s_cT, TILES)
            project_qpe(0)
            pe.wait_ge(s_wkvu, 64)
            project_v_mla(0)
            project_qk_mla(0)
            pe.wait_ge(s_kpsb, TILES)
            pair_mla(0, first=True)
            with pe.Fori(1, PAIRS - 1) as j:
                pair_mla(j)
            pair_mla(PAIRS - 1, last_pair=True)
            out_product(2 * PAIRS - 1, last_pair=True)
            peer(1)

        @block.scalar
        def _(act):
            for n in range(4):
                t, half = n // 2, n % 2
                act.wait_ge(s_xtr, n + 1)
                nc.scalar.activation(hT[:, 4 * half:4 * half + 4, t * P:(t + 1) * P],
                                     b_att[n % 2].rearrange("p (c n) -> p c n", c=4), ACT.Copy)\
                  .then_inc(s_xT, 1)

            def store_qk(jj, na):
                act.wait_ge(s_qkps, jj + 1)
                if na:
                    nc.scalar.activation(qk[:, 0, :].rearrange("p (r c) -> p r c", r=ROWS),
                                         rows_reversed(qk_ps[:, 0, :]), ACT.Copy, scale=NA_SCALE)
                else:
                    nc.scalar.activation(qk[:, 0, :], qk_ps[:, 0, :], ACT.Copy, scale=MLA_SCALE)
                nc.scalar.activation(qk[:, 1, :], qk_ps[:, 1, :], ACT.Copy).then_inc(s_qksb, 1)

            def store_v(jj):
                act.wait_ge(s_vps, jj + 1)
                nc.scalar.activation(v_sb[:, :, :], v_ps, ACT.Copy).then_inc(s_vsb, 1)

            def exps(jj, i, src):
                act.wait_ge(s_max, 2 * jj + i + 1)
                for t in range(TILES):
                    last = nc.scalar.activation(probs[i][:, t, :], src[:, t, :], ACT.Exp,
                                                bias=nmax[:, i, t:t + 1], accum_out=psum_row[:, i, t:t + 1])
                last.then_inc(s_exp, 1)

            def store_oT(jj, na):
                act.wait_ge(s_pv, 2 * jj + 2)
                if na:
                    nc.scalar.activation(oT[:, :].rearrange("p (r c) -> p r c", r=ROWS),
                                         rows_reversed(oT_ps), ACT.Copy).then_inc(s_oT, 1)
                else:
                    nc.scalar.activation(oT[:, :], oT_ps, ACT.Copy).then_inc(s_oT, 1)

            def pair(jj, src, na, last_pair=False):
                for i in range(2):
                    exps(jj, i, src[i])
                act.wait_ge(s_ptps, 2 * jj + 2)
                nc.scalar.activation(probsT[1][:, :, :].rearrange("p t n -> p (t n)"), b_att[1], ACT.Copy)\
                  .then_inc(s_ptsb, 1)
                if na and not last_pair:
                    store_qk(jj + 1, na)
                store_oT(jj, na)
                if not na and not last_pair:
                    store_qk(jj + 1, na)
                if not last_pair:
                    store_v(jj + 1)

            def mixer(first, src, na):
                if na:
                    store_qk(first, na)
                store_v(first)
                if not na:
                    store_qk(first, na)
                with act.Fori(first, first + PAIRS - 1) as jj:
                    pair(jj, src, na)
                pair(first + PAIRS - 1, src, na, True)

            mixer(0, [logits[i][:, :, :] for i in range(2)], True)

            act.wait_ge(s_ktr, 1)
            nc.scalar.activation(keysT[:, :, :], b_qk[:, :].rearrange("p (c n) -> p c n", c=2 * LAYERS),
                                 ACT.Copy).then_inc(s_kT, 1)
            act.wait_ge(s_small, 16 * 10)

            def norm_std(n, t):
                act.wait_ge(s_var, n + 1)
                nc.scalar.activation(ln_std[:, t:t + 1], ln_mv[:, t, 1:2], ACT.Sqrt, bias=eps_col[:, :])\
                  .then_inc(s_std, 1)

            def norm_store(n, cols, banks, t):
                for half in range(2):
                    act.wait_ge(s_tr, 2 * n + half + 1)
                    for c in range(4):
                        k = 4 * half + c
                        last = nc.scalar.activation(hT[:, k, t * P:(t + 1) * P], banks[half][:, c * P:(c + 1) * P],
                                                    ACT.Identity, scale=g_col[:, cols, k:k + 1],
                                                    bias=b_col[:, cols, k:k + 1])
                    last.then_inc(s_hT, 1)

            def latent_std(t):
                act.wait_ge(s_cps, t + 1)
                for s in range(2):
                    last = nc.scalar.activation(sq_junk[:, s, :], lat_ps[t][:, s * RANK:(s + 1) * RANK], ACT.Square,
                                                accum_out=c_ss[:, s:s + 1])
                last.then_inc(s_css, 1)
                act.wait_ge(s_cms, t + 1)
                nc.scalar.activation(c_std[:, :], c_ms[:, :], ACT.Sqrt).then_inc(s_cstd, 1)

            def store_queries(layer, h):
                act.wait_ge(s_qTps, layer * PH + h + 1)
                nc.scalar.activation(qT[:, :, :], qk_ps, ACT.Copy).then_inc(s_qTsb, 1)

            def gate_exp(layer, step, tiles=(0, 1)):
                act.wait_ge(s_bd, layer * CHOICES + choice_no(step, tiles) + 1)
                some = slice(tiles[0], tiles[-1] + 1)
                nc.scalar.activation(best_e[:, some, :], best_d[:, some, :], ACT.Exp).then_inc(s_be, 1)

            def weigh(layer, g, first=False):
                base = layer * GROUPS
                act.wait_ge(s_dot, dots_done((base + g + 1) * TOPK))
                nc.scalar.activation(act_hid[:, :], hid[:, :], ACT.Gelu).then_inc(s_gelu, 1)
                act.wait_ge(s_wts, base + g + 1)
                for k in range(TOPK):
                    if not first:
                        act.wait_ge(s_acc, products_done((base + g - 1) * TOPK + k + 1))
                    nc.scalar.activation(diag[:, k, :], ident[:, :], ACT.Copy, scale=wts[:, k:k + 1])\
                      .then_inc(s_diag, 1)

            def peer(layer):
                n = norm_no(layer, 0, 0)
                for t in range(TILES):
                    norm_std(n + t, t)
                for t in range(TILES):
                    norm_store(n + t, 2 * layer, mix_banks[t], t)
                for t in range(TILES):
                    act.wait_ge(s_q0ps if t == 0 else s_qTps, layer + 1 if t == 0 else layer * PH + 1)
                    nc.scalar.activation(qT[:, :, t * P:(t + 1) * P], first_q_ps[t], ACT.Copy)\
                      .then_inc(s_q0sb if t == 0 else s_qTsb, 1)
                gate_exp(layer, 0, (0,))
                gate_exp(layer, 1, (1,))
                store_queries(layer, 1)
                gate_exp(layer, 1, (0,))
                weigh(layer, 0, first=layer == 0)
                with act.Fori(1, PH - 1) as g:
                    store_queries(layer, g + 1)
                    gate_exp(layer, g + 1)
                    weigh(layer, g)
                gate_exp(layer, PH, (1,))
                weigh(layer, PH - 1)
                weigh(layer, PH)
                norm_std(n + 2, 0)
                if layer == 0:
                    norm_store(n + 2, 1, ffn_banks, 0)
                    latent_std(0)
                with act.Fori(PH + 1, GROUPS) as g:
                    weigh(layer, g)
                norm_std(n + 3, 1)
                if layer == 0:
                    norm_store(n + 3, 1, ffn_banks, 1)
                    latent_std(1)

            peer(0)
            mixer(PAIRS, [b_att[i].rearrange("p (t n) -> p t n", t=TILES) for i in range(2)], False)
            peer(1)

        @block.vector
        def _(dve):
            V = nc.vector
            dve.sem_inc(s_dot, RING)

            def softmax(jj, i, j=None, na=False):
                dve.wait_ge(s_sc, 2 * jj + i + 1)
                src = b_att[i].rearrange("p (t n) -> p t n", t=TILES)
                if na:
                    if i == 0:
                        dve.wait_ge(s_bias, jj + 1)
                    V.tensor_tensor(logits[i][:, :, :], src,
                                    bias[:, :, i, :, :].rearrange("p t r c -> p t (r c)"), ALU.add)\
                     .then_inc(s_badd, 1)
                    dve.drain()
                    src = logits[i][:, :, :]
                V.tensor_reduce(nmax[:, i, :], src, X, ALU.max, negate=True).then_inc(s_max, 1)

            def normalise(jj, i):
                dve.wait_ge(s_exp, 2 * jj + i + 1)
                V.reciprocal(rsum[:, i, :], psum_row[:, i, :])
                dve.drain()
                for t in range(TILES):
                    last = V.tensor_scalar(probs[i][:, t, :], probs[i][:, t, :], rsum[:, i, t:t + 1], None, ALU.mult)
                last.then_inc(s_prob, 1)

            def store_probsT(jj):
                dve.wait_ge(s_ptps, 2 * jj + 1)
                V.tensor_copy(probsT[0][:, :, :].rearrange("p t n -> p (t n)"), b_att[0]).then_inc(s_ptsb, 1)

            with dve.Fori(0, PAIRS) as j:
                for i in range(2):
                    softmax(j, i, na=True)
                for i in range(2):
                    normalise(j, i)
                store_probsT(j)

            def norm_stats(n, src, t):
                for c in range(2):
                    V.bn_stats(ln_stats[:, t, c, :], src[:, c, :])
                dve.drain()
                V.bn_aggr(ln_mv[:, t, :], ln_stats[:, t, :, :].rearrange("p a b -> p (a b)")).then_inc(s_var, 1)

            def norm_scale(n, src, t):
                dve.wait_ge(s_std, n + 1)
                V.reciprocal(ln_rstd[:, t:t + 1], ln_std[:, t:t + 1])
                dve.drain()
                V.tensor_scalar(nat[:, t, :].rearrange("p (c n) -> p c n", c=2), src,
                                ln_mv[:, t, 0:1], ln_rstd[:, t:t + 1], ALU.subtract, ALU.mult).then_inc(s_xhat, 1)

            def norm_affine(n, t):
                dve.wait_ge(s_rows, 32 * (n // 2 + 1))
                if n < norm_no(1, 1, 0):
                    dve.wait_ge(s_tr, 2 * n + 2)
                dve.drain()
                V.tensor_tensor(nat[:, t, :], nat[:, t, :], g_row[:, :], ALU.mult)
                dve.drain()
                V.tensor_tensor(nat[:, t, :], nat[:, t, :], b_row[:, :], ALU.add).then_inc(s_nat, 1)

            BOTH = (0, 1)

            def key_top16(layer, step, tiles=BOTH):
                dve.wait_ge(s_ks, layer * CHOICES + choice_no(step, tiles) + 1)
                dve.sem_inc(s_dstep, 1)
                some = slice(tiles[0], tiles[-1] + 1)
                both = [(t, c) for t in tiles for c in range(2)]
                for t, c in both:
                    V.max(key_top[:, t, c, 0:8], scores_ps[:, t, c, :])
                dve.drain()
                for t, c in both:
                    V.match_replace(key_left[:, t, c, :], key_top[:, t, c, 0:8], scores_ps[:, t, c, :], NEG)
                dve.drain()
                for t, c in both:
                    V.max(key_top[:, t, c, 8:16], key_left[:, t, c, :])
                for t, c in both:
                    V.max_index(key_idx[:, t, c, 0:8], key_top[:, t, c, 0:8], scores_ps[:, t, c, :])
                dve.drain()
                for t, c in both:
                    V.max_index(key_idx[:, t, c, 8:16], key_top[:, t, c, 8:16], key_left[:, t, c, :])
                dve.drain()
                V.tensor_copy(key_idxf[:, some, :, :], key_idx[:, some, :, :])

            def pair_top16(tiles=BOTH):
                some = slice(tiles[0], tiles[-1] + 1)
                for t in tiles:
                    V.tensor_tensor(cand[:, t, :, :], key_top[:, t, 0, :].unsqueeze(2).broadcast_to([P, TOPK, TOPK]),
                                    key_top[:, t, 1, :].unsqueeze(1).broadcast_to([P, TOPK, TOPK]), ALU.add)
                flat = [cand[:, t, :, :].rearrange("p a b -> p (a b)") for t in range(TILES)]
                dve.drain()
                for t in tiles:
                    V.max(best[:, t, 0:8], flat[t])
                dve.drain()
                for t in tiles:
                    V.match_replace(cand_left[:, t, :], best[:, t, 0:8], flat[t], NEG)
                for t in tiles:
                    V.max_index(pos[:, t, 0:8], best[:, t, 0:8], flat[t])
                dve.drain()
                for t in tiles:
                    V.max(best[:, t, 8:16], cand_left[:, t, :])
                dve.drain()
                for t in tiles:
                    V.max_index(pos[:, t, 8:16], best[:, t, 8:16], cand_left[:, t, :])
                V.tensor_tensor(best_d[:, some, :], best[:, some, :],
                                best[:, some, 0:1].broadcast_to([P, len(tiles), TOPK]), ALU.subtract).then_inc(s_bd, 1)

            def expert_numbers(layer, step, tiles=BOTH):
                some = slice(tiles[0], tiles[-1] + 1)
                halves = 2 * len(tiles)
                ranks = pos_abf[:, some, :, :].rearrange("p t c k -> p (t c) k")
                hits = hit[:, some, :, :, :].rearrange("p t c k n -> p (t c) k n")
                dve.drain()
                V.tensor_scalar(pos_ab[:, some, 0, :], pos[:, some, :], 4, None, ALU.logical_shift_right)
                V.tensor_scalar(pos_ab[:, some, 1, :], pos[:, some, :], TOPK - 1, None, ALU.bitwise_and)
                dve.drain()
                V.tensor_copy(pos_abf[:, some, :, :], pos_ab[:, some, :, :])
                dve.drain()
                V.tensor_tensor(hits.rearrange("p h k n -> p (h k) n"),
                                ranks.rearrange("p h k -> p (h k)").unsqueeze(2).broadcast_to([P, halves * TOPK, TOPK]),
                                iota16[:, :].unsqueeze(1).broadcast_to([P, halves * TOPK, TOPK]), ALU.is_equal)
                dve.drain()
                V.tensor_tensor(hits, hits, key_idxf[:, some, :, :].rearrange("p t c k -> p (t c) k").unsqueeze(2)
                                .broadcast_to([P, halves, TOPK, TOPK]), ALU.mult)
                dve.drain()
                V.tensor_reduce(pick[:, some, :, :].rearrange("p t c k -> p (t c k)"),
                                hits.rearrange("p h k n -> p (h k) n"), X, ALU.add)
                dve.drain()
                V.tensor_scalar(pick[:, some, 0, :], pick[:, some, 0, :], float(KEYS), float(layer * EXPERTS),
                                ALU.mult, ALU.add)
                dve.drain()
                for t in tiles:
                    V.tensor_tensor(expert[:, t, ds((step - t) * TOPK, TOPK)], pick[:, t, 0, :], pick[:, t, 1, :],
                                    ALU.add).then_inc(s_top[t], 1)

            def gates(layer, step, tiles=BOTH):
                some = slice(tiles[0], tiles[-1] + 1)
                dve.wait_ge(s_be, layer * CHOICES + choice_no(step, tiles) + 1)
                V.tensor_reduce(gate_s[:, some], best_e[:, some, :], X, ALU.add)
                dve.drain()
                V.reciprocal(gate_r[:, some], gate_s[:, some])
                dve.drain()
                for t in tiles:
                    V.tensor_scalar(gate[:, t, ds((step - t) * TOPK, TOPK)], best_e[:, t, :], gate_r[:, t:t + 1],
                                    None, ALU.mult)

            def dot(layer, g, k):
                b = k % RING
                base = layer * GROUPS
                dve.wait_ge(s_ug[b], 16 * ((base + g) * 2 + k // RING + 1))
                rows = u_rows[:, b, :].rearrange("p (c n) -> p c n", c=2)
                V.tensor_tensor_reduce(out=rows, in0=px, in1=rows, scale=1.0,
                                       scalar=0.0, op0=ALU.mult, op1=ALU.add, accum_out=hid[:, k:k + 1])\
                 .then_inc(s_dot, 1)

            gate_flat = gate[:, :, :].rearrange("p t n -> p (t n)")

            def weights(layer, g):
                dve.wait_ge(s_gelu, layer * GROUPS + g + 1)
                V.tensor_tensor(wts[:, :], act_hid[:, :], gate_flat[:, ds(g * TOPK, TOPK)], ALU.mult)\
                 .then_inc(s_wts, 1)

            def dots(layer, g, choice=None):
                for k in range(TOPK):
                    dot(layer, g, k)
                    if choice is None:
                        continue
                    step, tiles, at = choice
                    if k == at[0]:
                        key_top16(layer, step, tiles)
                    if k == at[1]:
                        dve.drain()
                        pair_top16(tiles)
                    if k == at[2]:
                        expert_numbers(layer, step, tiles)
                    if k == at[3]:
                        gates(layer, step, tiles)
                weights(layer, g)

            def load_px(t):
                dve.drain()
                V.tensor_copy(px, nat[:, t, :].rearrange("p (c n) -> p c n", c=2))
                dve.drain()

            def peer(layer):
                n = norm_no(layer, 0, 0)
                dve.wait_ge(s_y, (layer + 1) * PAIRS)
                for t in range(TILES):
                    norm_stats(n + t, y01[:, t, :, :], t)
                for t in range(TILES):
                    norm_scale(n + t, y01[:, t, :, :], t)
                for t in range(TILES):
                    norm_affine(n + t, t)
                dve.wait_ge(s_hT, 2 * (n + 1) + 2)
                load_px(0)
                for t in range(TILES):
                    key_top16(layer, t, (t,))
                    dve.drain()
                    pair_top16((t,))
                    expert_numbers(layer, t, (t,))
                    gates(layer, t, (t,))
                    dve.drain()
                dots(layer, 0, (1, (0,), (2, 4, 6, 7)))
                with dve.Fori(1, PH - 1) as g:
                    dots(layer, g, (g + 1, BOTH, (4, 7, 9, 11)))
                dots(layer, PH - 1, (PH, (1,), (5, 8, 10, 12)))
                load_px(1)
                dots(layer, PH)
                base = layer * GROUPS * TOPK
                dve.wait_ge(s_acc, products_done(base + PH * TOPK))
                norm_stats(n + 2, ffn[0], 0)
                norm_scale(n + 2, ffn[0], 0)
                norm_affine(n + 2, 0)
                if layer == 0:
                    latent_norm(0)
                    rope_k(0)
                    store_cT(0)
                with dve.Fori(PH + 1, GROUPS) as g:
                    dots(layer, g)
                dve.wait_ge(s_acc, products_done(base + GROUPS * TOPK))
                norm_stats(n + 3, ffn[1], 1)
                norm_scale(n + 3, ffn[1], 1)
                norm_affine(n + 3, 1)
                if layer == 0:
                    latent_norm(1)
                    store_cT(1)
                    rope_k(1)

            def rope(dst, src, cols, scale):
                V.scalar_tensor_tensor(out=rope_a[:, cols], in0=src[:, 0, :], scalar=scale,
                                       in1=cos_t[:, cols], op0=ALU.mult, op1=ALU.mult)
                V.scalar_tensor_tensor(out=rope_b[:, cols], in0=src[:, 1, :], scalar=scale,
                                       in1=sin_t[:, cols], op0=ALU.mult, op1=ALU.mult)
                dve.drain()
                return V.tensor_tensor(dst[:, cols], rope_a[:, cols], rope_b[:, cols], ALU.add)

            def rope_k(t):
                dve.wait_ge(s_kpps, t + 1)
                rope(kpe, kpe_ps[t], slice(t * P, (t + 1) * P), 1.0).then_inc(s_kpsb, 1)

            def rope_q(j):
                dve.drain()
                dve.wait_ge(s_peps, j + 1)
                rope(qpe, qk_ps[0:2 * ROPE, :, :], slice(0, TOK), MLA_SCALE).then_inc(s_pesb, 1)

            def latent_norm(t):
                dve.wait_ge(s_css, t + 1)
                V.tensor_scalar(c_ms[:, :], c_ss[:, :], 1.0 / RANK, EPS, ALU.mult, ALU.add).then_inc(s_cms, 1)
                dve.wait_ge(s_cstd, t + 1)
                V.reciprocal(c_rstd[:, :], c_std[:, :])
                dve.drain()
                for s in range(2):
                    last = V.tensor_scalar(cn[:, s * RK:(s + 1) * RK, :].rearrange("p c n -> p (c n)"),
                                           lat_ps[t][:, s * RANK:(s + 1) * RANK], c_rstd[:, s:s + 1], None, ALU.mult)
                last.then_inc(s_cn, 1)

            def store_cT(t):
                dve.wait_ge(s_ctr, t + 1)
                V.tensor_tensor(cT[:, :, t * P:(t + 1) * P], cT_ps.rearrange("p (c n) -> p c n", c=2 * RK),
                                norm_col[:, :].unsqueeze(2).broadcast_to([P, 2 * RK, P]), ALU.mult).then_inc(s_cT, 1)

            def pair_mla(j, last_pair=False):
                jj = PAIRS + j
                for i in range(2):
                    softmax(jj, i)
                for i in range(2):
                    normalise(jj, i)
                if not last_pair:
                    rope_q(j + 1)
                store_probsT(jj)

            dve.wait_ge(s_small, 16 * 10)
            peer(0)
            rope_q(0)
            with dve.Fori(0, PAIRS - 1) as j:
                pair_mla(j)
            pair_mla(PAIRS - 1, True)
            peer(1)


_INS = ['x', 'na_w_in', 'na_rel_bias', 'na_w_out', 'mla_w_in', 'mla_q_norm', 'mla_kv_norm', 'mla_w_q_up',
        'mla_w_kv_up', 'mla_w_out', 'peer_w_q', 'peer_sub_keys', 'peer_u', 'peer_v', 'ln_mix_g', 'ln_mix_b',
        'ln_ffn_g', 'ln_ffn_b']
_OUTS = [((1, TOK, D), 'float32')]


def kernel(**inputs):
    import numpy as _np
    import concourse.bacc as _bacc
    from concourse import mybir as _mybir
    from concourse.bass_utils import run_bass_kernel_spmd as _run

    half = ROPE // 2
    freq = (10000.0 ** (-_np.arange(half) * 2.0 / ROPE)).astype(_np.float32)
    angle = freq[:, None] * _np.arange(TOK, dtype=_np.float32)[None, :]
    cos, sin = _np.cos(angle), _np.sin(angle)
    tables = {'rope_cos': _np.concatenate([cos, cos, cos, cos], axis=0),
              'rope_sin': _np.concatenate([-sin, sin, -sin, sin], axis=0)}

    nc = _bacc.Bacc("TRN2", target_bir_lowering=False, num_devices=1)
    arrays, args = {}, []
    for name in _INS + list(tables):
        a = _np.ascontiguousarray(tables[name] if name in tables else inputs[name])
        arrays[f"in_{name}_dram"] = a
        args.append(nc.dram_tensor(f"in_{name}_dram", a.shape, _mybir.dt.from_np(a.dtype), kind="ExternalInput").ap())
    for i, (shape, dtype) in enumerate(_OUTS):
        dt = _mybir.dt.from_np(_np.dtype(dtype))
        args.append(nc.dram_tensor(f"out_{i}_dram", shape, dt, kind="ExternalOutput").ap())
    program(nc, *args)
    r = _run(nc, [arrays], core_ids=[0])
    return r.results[0]["out_0_dram"]
```
